# Optimizing a Trainium2 kernel written in Bass

```python
import math
import jax
import jax.numpy as jnp
from jax import lax
import numpy as np

D_MODEL = 1024
BATCH = 1
SEQ = 1024
DEPTH = 1
DEC_BATCH = 1
DEC_SEQ = 32
PAST_LEN = 2048

CHUNK = 64
N_META = 16
D_LRU = 512
LRU_BLOCKS = 8
LRU_BLOCK = D_LRU // LRU_BLOCKS
CONV_W = 4
LRU_C = 8.0
MLSTM_HEADS = 4
MLSTM_HEAD_DIM = 128
D_MLSTM = MLSTM_HEADS * MLSTM_HEAD_DIM
D_MIX = D_LRU + D_MLSTM
D_IN = 2 * D_LRU + 4 * D_MLSTM + 2 * MLSTM_HEADS
PEER_HEADS = 8
PEER_KEYS = 128
PEER_EXPERTS = PEER_KEYS * PEER_KEYS
PEER_QDIM = 256
PEER_HALF = PEER_QDIM // 2
PEER_TOPK = 16
PEER_BLOCK = 128
EPS = 1e-6

kernel_name = 'hymba_rglru_mlstm_peer_stream_step'

def rmsnorm(x, g):
    xf = x.astype(jnp.float32)
    y = xf * lax.rsqrt(jnp.mean(xf * xf, axis=-1, keepdims=True) + EPS)
    return (y * g.astype(jnp.float32)).astype(x.dtype)

def causal_conv(xl, hist, w, b):
    T = xl.shape[1]
    full = jnp.concatenate([hist.astype(xl.dtype), xl], axis=1)
    out = full[:, 0:T] * w[0]
    for j in range(1, CONV_W):
        out = out + full[:, j:j + T] * w[j]
    return out + b, full[:, -(CONV_W - 1):]

def rglru(xc, wa, ba, wx, bx, lam, h0, reset_first):
    B, T, _ = xc.shape
    xb = xc.reshape(B, T, LRU_BLOCKS, LRU_BLOCK)
    r = jax.nn.sigmoid(jnp.einsum('btni,nij->btnj', xb, wa).reshape(B, T, D_LRU).astype(jnp.float32) + ba.astype(jnp.float32))
    i = jax.nn.sigmoid(jnp.einsum('btni,nij->btnj', xb, wx).reshape(B, T, D_LRU).astype(jnp.float32) + bx.astype(jnp.float32))
    log_a = -LRU_C * r * jax.nn.softplus(-lam.astype(jnp.float32))
    a = jnp.exp(log_a)
    mult = jnp.sqrt(-jnp.expm1(2.0 * log_a))
    if reset_first:
        mult = mult.at[:, 0].set(1.0)
    bt = mult * i * xc.astype(jnp.float32)
    bt = bt.at[:, 0].add(a[:, 0] * h0)

    def comb(left, right):
        al, bl = left
        ar, br = right
        return al * ar, ar * bl + br

    _, h = lax.associative_scan(comb, (a, bt), axis=1)
    return h, h[:, -1]

def mlstm_chunk(carry, q, k, v, ig, lf):
    c_prev, n_prev, m_prev = carry
    L = q.shape[1]
    b = jnp.cumsum(lf, axis=1)
    causal = jnp.tril(jnp.ones((L, L), dtype=bool))[None, :, :, None]
    d = b[:, :, None, :] - b[:, None, :, :] + ig[:, None, :, :]
    d = jnp.where(causal, d, -jnp.inf)
    inter = b + m_prev[:, None, :]
    m_tok = jnp.maximum(inter, jnp.max(d, axis=2))
    w = jnp.exp(d - m_tok[:, :, None, :])
    s = jnp.einsum('blhd,bshd->blsh', q, k) * w
    decay = jnp.exp(inter - m_tok)
    num = decay[..., None] * jnp.einsum('blhd,bhde->blhe', q, c_prev) + jnp.einsum('blsh,bshe->blhe', s, v)
    den = decay * jnp.einsum('blhd,bhd->blh', q, n_prev) + jnp.sum(s, axis=2)
    h = num / jnp.maximum(jnp.abs(den), jnp.exp(-m_tok))[..., None]
    m_new = m_tok[:, -1]
    dec_prev = jnp.exp(b[:, -1] + m_prev - m_new)
    w_end = jnp.exp(b[:, -1:, :] - b + ig - m_new[:, None, :])
    c_new = dec_prev[..., None, None] * c_prev + jnp.einsum('bsh,bshd,bshe->bhde', w_end, k, v)
    n_new = dec_prev[..., None] * n_prev + jnp.einsum('bsh,bshd->bhd', w_end, k)
    return (c_new, n_new, m_new), h

def mlstm_run(carry, q, k, v, ig, lf, lead):
    B = q.shape[0]
    outs = []
    if lead > 0:
        carry, h_lead = mlstm_chunk(carry, q[:, :lead], k[:, :lead], v[:, :lead], ig[:, :lead], lf[:, :lead])
        outs.append(h_lead)
        q, k, v, ig, lf = q[:, lead:], k[:, lead:], v[:, lead:], ig[:, lead:], lf[:, lead:]
    T = q.shape[1]
    if T <= CHUNK:
        carry, h = mlstm_chunk(carry, q, k, v, ig, lf)
    else:
        n_chunks = T // CHUNK

        def to_chunks(t):
            return jnp.moveaxis(t.reshape((B, n_chunks, CHUNK) + t.shape[2:]), 1, 0)

        def step(c, xs):
            return mlstm_chunk(c, *xs)

        carry, h = lax.scan(step, carry, (to_chunks(q), to_chunks(k), to_chunks(v), to_chunks(ig), to_chunks(lf)))
        h = jnp.moveaxis(h, 0, 1).reshape((B, T) + h.shape[3:])
    outs.append(h)
    return carry, jnp.concatenate(outs, axis=1)

def mixer(xn, conv_hist, h0, c0, n0, m0, w_in, b_gates, conv_w, conv_b, lru_wa, lru_ba, lru_wx, lru_bx,
          lru_lambda, mlstm_norm, w_out, reset_first, lead):
    B, T, _ = xn.shape
    f32 = jnp.float32
    proj = xn @ w_in
    cuts = [D_LRU, 2 * D_LRU, 2 * D_LRU + D_MLSTM, 2 * D_LRU + 2 * D_MLSTM,
            2 * D_LRU + 3 * D_MLSTM, 2 * D_LRU + 4 * D_MLSTM]
    xl, gl, q, k, v, o, gates = jnp.split(proj, cuts, axis=-1)
    xc, conv_new = causal_conv(xl, conv_hist, conv_w, conv_b)
    h_lru, h_last = rglru(xc, lru_wa, lru_ba, lru_wx, lru_bx, lru_lambda, h0.astype(f32), reset_first)
    y_lru = h_lru * jax.nn.gelu(gl.astype(f32))
    hd = (B, T, MLSTM_HEADS, MLSTM_HEAD_DIM)
    qf = q.reshape(hd).astype(f32)
    kf = k.reshape(hd).astype(f32) * (MLSTM_HEAD_DIM ** -0.5)
    vf = v.reshape(hd).astype(f32)
    g = gates.astype(f32) + b_gates.astype(f32)
    ig = g[..., :MLSTM_HEADS]
    lf = jax.nn.log_sigmoid(g[..., MLSTM_HEADS:])
    carry0 = (c0.astype(f32), n0.astype(f32), m0.astype(f32))
    (c1, n1, m1), hm = mlstm_run(carry0, qf, kf, vf, ig, lf, lead)
    hm = hm * lax.rsqrt(jnp.mean(hm * hm, axis=-1, keepdims=True) + EPS)
    y_m = hm.reshape(B, T, D_MLSTM) * mlstm_norm.astype(f32) * jax.nn.sigmoid(o.astype(f32))
    y = jnp.concatenate([y_lru, y_m], axis=-1).astype(xn.dtype) @ w_out
    return y, (conv_new, h_last, c1, n1, m1)

def peer(xn, wq, keys1, keys2, u_tab, v_tab):
    B, T, D = xn.shape
    flat = xn.reshape(B * T, D)
    n_tok = B * T
    n_blk = -(-n_tok // PEER_BLOCK)
    flat = jnp.pad(flat, ((0, n_blk * PEER_BLOCK - n_tok), (0, 0))).reshape(n_blk, PEER_BLOCK, D)

    def block(xb):
        qh = (xb @ wq).reshape(PEER_BLOCK, PEER_HEADS, 2, PEER_HALF)
        s1 = jnp.einsum('thd,nd->thn', qh[:, :, 0], keys1).astype(jnp.float32)
        s2 = jnp.einsum('thd,nd->thn', qh[:, :, 1], keys2).astype(jnp.float32)
        v1, i1 = lax.top_k(s1, PEER_TOPK)
        v2, i2 = lax.top_k(s2, PEER_TOPK)
        cand = (v1[..., :, None] + v2[..., None, :]).reshape(PEER_BLOCK, PEER_HEADS, PEER_TOPK * PEER_TOPK)
        sc, ci = lax.top_k(cand, PEER_TOPK)
        e = (jnp.take_along_axis(i1, ci // PEER_TOPK, axis=-1) * PEER_KEYS
             + jnp.take_along_axis(i2, ci % PEER_TOPK, axis=-1))
        gate = jax.nn.softmax(sc, axis=-1)
        act = jax.nn.gelu(jnp.einsum('td,thkd->thk', xb, u_tab[e]).astype(jnp.float32)) * gate
        return jnp.einsum('thk,thkd->td', act.astype(xb.dtype), v_tab[e])

    out = lax.map(block, flat).reshape(n_blk * PEER_BLOCK, D)[:n_tok]
    return out.reshape(B, T, D)

def setup_inputs(seed: int = 0) -> dict:
    key = jax.random.key(seed)
    ks = jax.random.split(key, 32)
    f32 = jnp.float32

    def nrm(k, shape, scale):
        return jax.random.normal(k, shape, f32) * scale

    u = jax.random.uniform(ks[0], (DEPTH, D_LRU), f32, 0.9, 0.999)
    s = u ** (1.0 / LRU_C)
    lru_lambda = jnp.log(s) - jnp.log1p(-s)
    b_i = nrm(ks[1], (DEPTH, MLSTM_HEADS), 0.1)
    b_f = jnp.linspace(3.0, 6.0, MLSTM_HEADS, dtype=f32)[None, :] + nrm(ks[2], (DEPTH, MLSTM_HEADS), 0.1)
    return {
        'x_prompt': nrm(ks[3], (BATCH, SEQ, D_MODEL), 1.0),
        'x_sample': nrm(ks[4], (DEC_BATCH, DEC_SEQ, D_MODEL), 1.0),
        'state_conv': nrm(ks[5], (DEPTH, DEC_BATCH, CONV_W - 1, D_LRU), 1.0),
        'state_lru': nrm(ks[6], (DEPTH, DEC_BATCH, D_LRU), 0.5),
        'state_mlstm_c': nrm(ks[7], (DEPTH, DEC_BATCH, MLSTM_HEADS, MLSTM_HEAD_DIM, MLSTM_HEAD_DIM), 0.1),
        'state_mlstm_n': nrm(ks[8], (DEPTH, DEC_BATCH, MLSTM_HEADS, MLSTM_HEAD_DIM), 0.5),
        'state_mlstm_m': nrm(ks[9], (DEPTH, DEC_BATCH, MLSTM_HEADS), 1.0),
        'meta_tokens': nrm(ks[10], (N_META, D_MODEL), 1.0),
        'w_in': nrm(ks[11], (DEPTH, D_MODEL, D_IN), D_MODEL ** -0.5),
        'b_gates': jnp.concatenate([b_i, b_f], axis=-1),
        'conv_w': nrm(ks[12], (DEPTH, CONV_W, D_LRU), CONV_W ** -0.5),
        'conv_b': nrm(ks[13], (DEPTH, D_LRU), 0.02),
        'lru_wa': nrm(ks[14], (DEPTH, LRU_BLOCKS, LRU_BLOCK, LRU_BLOCK), LRU_BLOCK ** -0.5),
        'lru_ba': nrm(ks[15], (DEPTH, D_LRU), 0.02),
        'lru_wx': nrm(ks[16], (DEPTH, LRU_BLOCKS, LRU_BLOCK, LRU_BLOCK), LRU_BLOCK ** -0.5),
        'lru_bx': nrm(ks[17], (DEPTH, D_LRU), 0.02),
        'lru_lambda': lru_lambda,
        'mlstm_norm': 1.0 + nrm(ks[18], (DEPTH, D_MLSTM), 0.01),
        'w_out': nrm(ks[19], (DEPTH, D_MIX, D_MODEL), D_MIX ** -0.5),
        'norm_mix': 1.0 + nrm(ks[20], (DEPTH, D_MODEL), 0.01),
        'norm_ffn': 1.0 + nrm(ks[21], (DEPTH, D_MODEL), 0.01),
        'peer_wq': nrm(ks[22], (DEPTH, D_MODEL, PEER_HEADS * PEER_QDIM), D_MODEL ** -0.5),
        'peer_keys1': nrm(ks[23], (DEPTH, PEER_KEYS, PEER_HALF), PEER_HALF ** -0.5),
        'peer_keys2': nrm(ks[24], (DEPTH, PEER_KEYS, PEER_HALF), PEER_HALF ** -0.5),
        'peer_u': nrm(ks[25], (DEPTH, PEER_EXPERTS, D_MODEL), D_MODEL ** -0.5),
        'peer_v': nrm(ks[26], (DEPTH, PEER_EXPERTS, D_MODEL), PEER_HEADS ** -0.5),
        'norm_final': 1.0 + nrm(ks[27], (D_MODEL,), 0.01),
    }

def reference(x_prompt, x_sample, state_conv, state_lru, state_mlstm_c, state_mlstm_n, state_mlstm_m,
              meta_tokens, w_in, b_gates, conv_w, conv_b, lru_wa, lru_ba, lru_wx, lru_bx, lru_lambda,
              mlstm_norm, w_out, norm_mix, norm_ffn, peer_wq, peer_keys1, peer_keys2, peer_u, peer_v,
              norm_final):
    f32 = jnp.float32
    B = x_prompt.shape[0]
    meta = jnp.broadcast_to(meta_tokens[None].astype(x_prompt.dtype), (B, N_META, D_MODEL))
    hp = jnp.concatenate([meta, x_prompt], axis=1)
    hs = x_sample
    zero_conv = jnp.zeros((B, CONV_W - 1, D_LRU), x_prompt.dtype)
    zero_h = jnp.zeros((B, D_LRU), f32)
    zero_c = jnp.zeros((B, MLSTM_HEADS, MLSTM_HEAD_DIM, MLSTM_HEAD_DIM), f32)
    zero_n = jnp.zeros((B, MLSTM_HEADS, MLSTM_HEAD_DIM), f32)
    zero_m = jnp.zeros((B, MLSTM_HEADS), f32)
    p_states = []
    s_states = []
    for l in range(DEPTH):
        lw = (w_in[l], b_gates[l], conv_w[l], conv_b[l], lru_wa[l], lru_ba[l], lru_wx[l], lru_bx[l],
              lru_lambda[l], mlstm_norm[l], w_out[l])
        pw = (peer_wq[l], peer_keys1[l], peer_keys2[l], peer_u[l], peer_v[l])
        yp, stp = mixer(rmsnorm(hp, norm_mix[l]), zero_conv, zero_h, zero_c, zero_n, zero_m, *lw,
                        reset_first=True, lead=N_META)
        hp = hp + yp
        hp = hp + peer(rmsnorm(hp, norm_ffn[l]), *pw)
        ys, sts = mixer(rmsnorm(hs, norm_mix[l]), state_conv[l], state_lru[l], state_mlstm_c[l],
                        state_mlstm_n[l], state_mlstm_m[l], *lw, reset_first=False, lead=0)
        hs = hs + ys
        hs = hs + peer(rmsnorm(hs, norm_ffn[l]), *pw)
        p_states.append(stp)
        s_states.append(sts)
    y_prompt = rmsnorm(hp[:, N_META:], norm_final)
    y_sample = rmsnorm(hs, norm_final)
    conv_p = jnp.stack([st[0] for st in p_states])
    lru_p = jnp.stack([st[1] for st in p_states])
    c_p = jnp.stack([st[2] for st in p_states])
    n_p = jnp.stack([st[3] for st in p_states])
    m_p = jnp.stack([st[4] for st in p_states])
    conv_s = jnp.stack([st[0] for st in s_states])
    lru_s = jnp.stack([st[1] for st in s_states])
    c_s = jnp.stack([st[2] for st in s_states])
    n_s = jnp.stack([st[3] for st in s_states])
    m_s = jnp.stack([st[4] for st in s_states])
    return (y_prompt, y_sample, conv_p, lru_p, c_p, n_p, m_p, conv_s, lru_s, c_s, n_s, m_s)


_drawn_inputs = setup_inputs


def setup_inputs(seed=0):
    import zlib

    import numpy as np

    out = dict(_drawn_inputs(seed))
    spreads = {}
    factors = {'lru_ba': 8.0,
     'lru_bx': 6.818,
     'mlstm_norm': 27.238,
     'norm_mix': 3.183,
     'norm_ffn': 15.016,
     'norm_final': 38.593,
     'state_mlstm_n': 8.0,
     'state_mlstm_m': 5.001}
    for name, (base, spread) in spreads.items():
        noise = np.random.default_rng([zlib.crc32(name.encode()), seed]).standard_normal(out[name].shape)
        drawn = base * np.exp(spread * noise) if base else spread * noise
        out[name] = jnp.asarray(drawn.astype(out[name].dtype))
    for name, factor in factors.items():
        out[name] = (out[name] * factor).astype(out[name].dtype)
    return out
```

```python
import numpy as np
import concourse.bass as bass
from concourse import mybir
from contextlib import ExitStack

D_MODEL = 1024
SEQ = 1024
SAMPLE = 32
META = 16
D_LRU = 512
HEADS = 4
HEAD = 128
CONV_W = 4
D_IN = 2 * D_LRU + 4 * HEADS * HEAD + 2 * HEADS
PEER_HEADS = 8
TOPK = 16
P = 128
CM = D_MODEL // P
FT = D_LRU // P
BLOCKS = SEQ // P
EPS = 1e-6
GELU_CUBIC = 0.044715
GELU_SCALE = -2.0 * (2.0 / np.pi) ** 0.5
COPIES = P // SAMPLE
RING = 8
DIAGS = 4
VECS = 5 * FT + CM
MASKED = -1.0e30

TICKS = PEER_HEADS * TOPK + TOPK
T_LOAD, T_NORM, T_XT, T_XT_OUT = 2, 5, 8, 9
T_XL, T_GATES, T_GL = 12, 16, 17
T_CONV, T_LRU = 20, 25
T_Q, T_K, T_V = 22, 27, 33
T_ROWS = 20
T_O = 41
T_CHUNK = 44
T_OUT = 64
T_NORM2 = 76
T_QUERY = 82
T_TOPK = 86
TOPK_TICKS = 5


def spread(ap, axis, n):
    shape = list(ap.shape)
    shape[axis] = n
    return ap.to_broadcast(shape)


def is_count(v, number):
    return isinstance(v, int) and v == number


def program(nc, x_prompt, x_sample, meta, w_in, vecs, conv_w, b_gates, lru_wa, lru_wx, w_out, ffn_row, final_row,
            wq, keys, peer_u, peer_v, conv0, lru0, c0, m0, y_prompt, y_sample, conv_out, lru_out, c_out, m_out):
    fp32, u32 = mybir.dt.float32, mybir.dt.uint32
    ALU, ACT, AX = mybir.AluOpType, mybir.ActivationFunctionType, mybir.AxisListType
    ctx = ExitStack()
    with ctx:
        def sb(name, shape, dt=fp32):
            return ctx.enter_context(nc.sbuf_tensor(name, shape, dt))

        def sem(name):
            return ctx.enter_context(nc.semaphore(name))

        win = sb("win", [P, CM, D_IN])
        wout = sb("wout", [P, CM, D_MODEL])
        wa = sb("wa", [P, FT, P])
        wx = sb("wx", [P, FT, P])
        keysT = sb("keysT", [P, 2, P])
        ffn_bc = sb("ffn_bc", [P, D_MODEL])
        final_bc = sb("final_bc", [P, D_MODEL])
        vec = sb("vec", [P, VECS])
        cw = sb("cw", [P, FT, CONV_W])
        bg = sb("bg", [HEADS, 2])
        ident = sb("ident", [P, P])
        mask = sb("mask", [P, P])
        rep = sb("rep", [P, SAMPLE])
        iota = sb("iota", [P, TOPK])
        ones4 = sb("ones4", [HEADS, P])
        eps = sb("eps", [P, 1])
        neg = sb("neg", [P, 2 * FT])
        nbf = sb("nbf", [HEADS, 1])
        decay_c = sb("decay_c", [P, 2 * FT])
        sp_t = sb("sp_t", [P, 6, FT])
        ring = sb("ring", [P, RING, D_MODEL])
        xcur = sb("xcur", [P, D_MODEL])
        idx = sb("idx", [P, PEER_HEADS * TOPK], u32)
        gate = sb("gate", [P, PEER_HEADS * TOPK])
        dots = sb("dots", [P, PEER_HEADS * TOPK])
        coef = sb("coef", [P, PEER_HEADS * TOPK])
        gl_a = sb("gl_a", [P, TOPK])
        gl_b = sb("gl_b", [P, TOPK])
        diag = sb("diag", [P, DIAGS, P])
        idx_n = sb("idx_n", [P, PEER_HEADS * TOPK], u32)
        gate_n = sb("gate_n", [P, PEER_HEADS, TOPK])
        h = sb("h", [P, D_MODEL])
        xn = sb("xn", [P, D_MODEL])
        xT = sb("xT", [P, CM, P])
        xl = sb("xl", [P, FT, CONV_W - 1 + P])
        G = sb("G", [P, FT, P])
        xc = sb("xc", [P, FT, P])
        qk = sb("qk", [P, 2 * FT, P])
        t34 = sb("t34", [P, 2 * FT, P])
        vt = sb("vt", [P, HEADS, HEAD + 1])
        kw = sb("kw", [P, HEADS, HEAD])
        C = sb("C", [P, HEADS, HEAD + 1])
        hst = sb("hst", [P, FT])
        mst = sb("mst", [HEADS, 1])
        rows_hi = sb("rows_hi", [HEADS, 2, P])
        dg4 = sb("dg4", [HEADS, HEADS])
        cols = sb("cols", [P, 5, HEADS])
        den = sb("den", [P, HEADS])
        stat = sb("stat", [P, 9])
        hstat = sb("hstat", [P, HEADS])
        tops = sb("tops", [P, 2, TOPK])
        topi = sb("topi", [P, 2, TOPK], u32)
        ci = sb("ci", [P, 3, TOPK], u32)
        eh = sb("eh", [P, 2, TOPK])
        gsum = sb("gsum", [P, 2, PEER_HEADS])
        qT, kT = qk[:, 0:FT, :], qk[:, FT:2 * FT, :]
        sigo = qk[:, 0:FT, :]
        t3, t4 = t34[:, 0:FT, :], t34[:, FT:2 * FT, :]
        t1 = xn[:, 0:512].rearrange("p (f t) -> p f t", f=FT)
        t2 = xn[:, 512:1024].rearrange("p (f t) -> p f t", f=FT)
        ba, bx, lam, mnorm, convb = (slice(FT * a, FT * a + FT) for a in range(5))
        nmix = slice(5 * FT, 5 * FT + CM)
        wq_buf = [qk, t34]
        q2 = G
        kflat = kw[:, :, :].rearrange("p h d -> p (h d)")
        rows = [kflat[0:HEADS, P * r:P * r + P] for r in range(4)] + [rows_hi[:, 0, :], rows_hi[:, 1, :]]
        tk_s = kflat[:, 0:256]
        tk_c = kflat[:, 256:512]
        acc = ctx.enter_context(nc.psum_tensor("acc", [P, D_MODEL], fp32))
        bank = [ctx.enter_context(nc.psum_tensor(f"bank{b}", [P, 512], fp32)) for b in range(6)]
        bA, bB, bC, bD, bE, bF = bank

        def by4(b):
            return b[:, :].rearrange("p (f t) -> p f t", f=FT)

        def pair(b):
            return b[:, 0:2 * (HEAD + 1)].rearrange("p (h e) -> p h e", h=2)

        s_small = sem("s_small")
        s_state_in = sem("s_state_in")
        s_win = [sem(f"s_win{g}") for g in range(7)]
        s_wout = sem("s_wout")
        s_x = sem("s_x")
        s_wq = [sem("s_wq0"), sem("s_wq1")]
        s_row = [sem(f"s_row{r}") for r in range(RING)]
        s_y_out = sem("s_y_out")
        s_state_out = sem("s_state_out")
        s_zero = sem("s_zero")
        s_blocks = sem("s_blocks")
        s_const = sem("s_const")
        s_pool = sem("s_pool")
        s_setup = sem("s_setup")
        s_setup_e, s_setup_l, s_setup_a = sem("s_setup_e"), sem("s_setup_l"), sem("s_setup_a")
        s_reset = sem("s_reset")
        s_idx_cur, s_xcur, s_gate_cur = sem("s_idx_cur"), sem("s_xcur"), sem("s_gate_cur")
        s_dot, s_arg, s_gexp, s_coef = sem("s_dot"), sem("s_arg"), sem("s_gexp"), sem("s_coef")
        s_diag, s_vsum, s_acc0 = sem("s_diag"), sem("s_vsum"), sem("s_acc0")
        s_acc_out, s_rstd_y, s_y = sem("s_acc_out"), sem("s_rstd_y"), sem("s_y")
        s_xn, s_xt_ps, s_xt = sem("s_xn"), sem("s_xt_ps"), sem("s_xt")
        s_xl_ps, s_xl, s_xc = sem("s_xl_ps"), sem("s_xl"), sem("s_xc")
        s_gl_ps, s_gl, s_gl_arg, s_gl_exp = sem("s_gl_ps"), sem("s_gl"), sem("s_gl_arg"), sem("s_gl_exp")
        s_ri_ps, s_ri_exp, s_r, s_a, s_m2, s_mult, s_lru = (sem(f"s_{n}") for n in ("ri_ps", "ri_exp", "r", "a", "m2", "mult", "lru"))
        s_q_ps, s_q, s_k_ps, s_k, s_v_ps, s_v = (sem(f"s_{n}") for n in ("q_ps", "q", "k_ps", "k", "v_ps", "v"))
        s_g_ps, s_fneg, s_fabs, s_fln, s_mrow, s_rows = (sem(f"s_{n}") for n in ("g_ps", "fneg", "fabs", "fln", "mrow", "rows"))
        s_dg, s_cols_ps, s_cols, s_bc_ps, s_qd, s_wmask, s_w = (sem(f"s_{n}") for n in ("dg", "cols_ps", "cols", "bc_ps", "qd", "wmask", "w"))
        s_kt_ps, s_kw, s_s_ps, s_p, s_num_ps, s_num, s_c_ps, s_c = (sem(f"s_{n}") for n in ("kt_ps", "kw", "s_ps", "p", "num_ps", "num", "c_ps", "c"))
        s_o_ps, s_o, s_hsq, s_hrs, s_ym, s_ym_ps, s_ymT = (sem(f"s_{n}") for n in ("o_ps", "o", "hsq", "hrs", "ym", "ym_ps", "ymT"))
        s_out_ps, s_h2, s_rstd2, s_xn2, s_x2_ps, s_x2 = (sem(f"s_{n}") for n in ("out_ps", "h2", "rstd2", "xn2", "x2_ps", "x2"))
        s_qp_ps, s_q2, s_score, s_topk, s_shift, s_gate_e, s_sel = (sem(f"s_{n}") for n in ("qp_ps", "q2", "score", "topk", "shift", "gate_e", "sel"))
        s_pool_turn, s_dve_turn = sem("s_pool_turn"), sem("s_dve_turn")
        s_dve, s_act = sem("s_dve"), sem("s_act")

        def experts_before(w, sample):
            return 0 if sample else w * P - (P - SAMPLE)

        def groups_before(w, sample):
            return 0 if sample else w * PEER_HEADS - (PEER_HEADS - SAMPLE // TOPK)

        def gathers_before(w, sample):
            return 0 if sample else w * (2 * P // RING) - 2 * (P - SAMPLE) // RING

        def n_experts(sample):
            return SAMPLE if sample else P

        def u_place(t):
            return t if t < TOPK else 2 * t - TOPK

        def v_place(j, sample):
            n = n_experts(sample)
            return 2 * j + TOPK + 1 if j < n - TOPK else j + n

        block = ctx.enter_context(nc.Block())

        @block.sync
        def _(sp):
            w_cols = w_in.rearrange("(c p) n -> p c n", p=P)

            def load_win(g):
                lo, hi = 512 * g, min(512 * g + 512, D_IN)
                sp.dma_start(win[:, :, lo:hi], w_cols[:, :, lo:hi]).then_inc(s_win[g], 16)

            def load_wq(w):
                for ft in range(2 * PEER_HEADS):
                    if ft < 2:
                        sp.wait_ge(s_ym_ps, w + 1)
                    else:
                        sp.wait_ge(s_qp_ps, w * 16 + ft - 1)
                    sp.dma_start(wq_buf[ft % 2][:, :, :], wq[ft]).then_inc(s_wq[ft % 2], 16)

            def store_states(stream, v, w):
                sp.wait_ge(s_lru, v + 1)
                sp.dma_start(conv_out[stream], xl[:, :, 0:CONV_W - 1]).then_inc(s_state_out, 16)
                sp.dma_start(lru_out[stream], hst[:, :]).then_inc(s_state_out, 16)
                sp.wait_ge(s_c, v + 1)
                sp.dma_start(c_out[stream], C[:, :, :]).then_inc(s_state_out, 16)
                sp.dma_start(m_out[stream], mst[:, :]).then_inc(s_state_out, 16)

            def store_y(w, rows_n, dst):
                sp.wait_ge(s_y, w + 1)
                sp.dma_start(dst, xT[0:rows_n, :, :].rearrange("p c t -> p (c t)")).then_inc(s_y_out, 16)

            sp.dma_start(h[0:SAMPLE, :], x_sample).then_inc(s_x, 16)
            sp.dma_start(vec[:, :], vecs).then_inc(s_small, 16)
            sp.dma_start(cw[:, :, :], conv_w).then_inc(s_small, 16)
            sp.dma_start(bg[:, :], b_gates).then_inc(s_small, 16)
            sp.dma_start(keysT[:, :, :], keys).then_inc(s_small, 16)
            sp.dma_start(ffn_bc[:, :], spread(ffn_row, 0, P)).then_inc(s_small, 16)
            sp.dma_start(final_bc[:, :], spread(final_row, 0, P)).then_inc(s_small, 16)
            load_win(0)
            sp.dma_start(xl[:, :, 0:CONV_W - 1], conv0).then_inc(s_state_in, 16)
            sp.dma_start(hst[:, :], lru0).then_inc(s_state_in, 16)
            sp.dma_start(C[:, :, :], c0).then_inc(s_state_in, 16)
            sp.dma_start(mst[:, :], m0).then_inc(s_state_in, 16)
            sp.wait_ge(s_zero, 2)
            for half in range(2):
                lo = half * 64
                sp.dma_start(wa[lo:lo + 64, :, lo:lo + 64], lru_wa[half]).then_inc(s_blocks, 16)
                sp.dma_start(wx[lo:lo + 64, :, lo:lo + 64], lru_wx[half]).then_inc(s_blocks, 16)
            for g in (6, 1, 2, 3, 4, 5):
                load_win(g)
            sp.dma_start(wout[:, :, :], w_out.rearrange("(c p) n -> p c n", p=P)).then_inc(s_wout, 16)
            load_wq(0)
            store_states(0, 0, 0)
            sp.wait_ge(s_acc0, 1)
            sp.dma_start(h[0:META, :], meta).then_inc(s_x, 16)
            sp.wait_ge(s_xn, 2)
            sp.dma_start(h[:, :], x_prompt[0:P, :]).then_inc(s_x, 16)
            load_wq(1)
            store_y(0, SAMPLE, y_sample)
            with sp.Fori(0, BLOCKS - 1) as i:
                sp.wait_ge(s_acc0, i + 2)
                sp.dma_start(h[:, :], x_prompt[bass.ds(i * P + P, P), :]).then_inc(s_x, 16)
                load_wq(i + 2)
                store_y(i + 1, P, y_prompt[bass.ds(i * P, P), :])
            store_states(1, BLOCKS + 1, BLOCKS)
            store_y(BLOCKS, P, y_prompt[(BLOCKS - 1) * P:BLOCKS * P, :])
            sp.wait_ge(s_state_out, 128)
            sp.wait_ge(s_y_out, 16 * (BLOCKS + 1))

        @block.gpsimd
        def _(pool):
            pool.memset(wa[:, :, :], 0.0).then_inc(s_zero, 1)
            pool.memset(wx[:, :, :], 0.0).then_inc(s_zero, 1)
            pool.memset(ident[:, :], 0.0).then_inc(s_pool, 1)
            pool.memset(mask[:, :], 0.0).then_inc(s_pool, 1)
            pool.memset(rep[:, :], 0.0).then_inc(s_pool, 1)
            pool.memset(ones4[:, :], 1.0).then_inc(s_const, 1)
            pool.memset(eps[:, :], EPS).then_inc(s_const, 1)
            pool.memset(vt[:, :, HEAD:HEAD + 1], 1.0).then_inc(s_const, 1)
            pool.iota(iota[:, :], pattern=[[1, TOPK]], base=0, channel_multiplier=0,
                      allow_small_or_imprecise_dtypes=True).then_inc(s_const, 1)
            pool.wait_ge(s_pool, 3)
            pool.affine_select(out=ident[:, :], in_=ident[:, :], compare_op=ALU.not_equal, fill=1.0, base=0,
                               pattern=[[-1, P]], channel_multiplier=1).then_inc(s_const, 1)
            pool.affine_select(out=mask[:, :], in_=mask[:, :], compare_op=ALU.is_ge, fill=MASKED, base=0,
                               pattern=[[1, P]], channel_multiplier=-1).then_inc(s_const, 1)
            for q in range(COPIES):
                pool.affine_select(out=rep[:, :], in_=rep[:, :], compare_op=ALU.not_equal, fill=1.0,
                                   base=-SAMPLE * q, pattern=[[-1, SAMPLE]], channel_multiplier=1).then_inc(s_pool, 1)
                pool.wait_ge(s_pool, 4 + q)
            pool.memset(diag[:, :, :], 0.0).then_inc(s_const, 1)

            def copy_idx(w, sample, part):
                if not sample:
                    for r in range(RING):
                        pool.wait_ge(s_row[r], gathers_before(w, sample) * 16 - (2 * 16 if part == 0 else 0))
                        pool.sem_inc(s_pool_turn, 1)
                lo, hi = (0, TOPK) if part == 0 else (TOPK, n_experts(sample))
                if sample:
                    for q in range(COPIES):
                        last = pool.tensor_copy(
                            idx[SAMPLE * q:SAMPLE * q + SAMPLE, lo:hi],
                            idx_n[0:SAMPLE, :].rearrange("p (c q) -> p c q", q=COPIES)[:, lo:hi, q])
                else:
                    last = pool.tensor_copy(idx[:, lo:hi], idx_n[:, lo:hi])
                last.then_inc(s_idx_cur, 1)
                pool.wait_ge(s_idx_cur, 2 * w + 1 + part)

            def gathers(w, sample):
                n = n_experts(sample)
                before, per_slot = experts_before(w, sample), gathers_before(w, sample)
                pool.wait_ge(s_sel, w + 1)
                pool.sem_inc(s_pool_turn, 1)
                copy_idx(w, sample, 0)
                order = sorted([(u_place(t), 0, t) for t in range(n)] + [(v_place(j, sample), 1, j) for j in range(n)])
                for place, is_v, e in order:
                    if place == TOPK:
                        copy_idx(w, sample, 1)
                    if place >= RING:
                        used = [o for o in order if o[0] == place - RING][0]
                        pool.wait_ge(s_vsum if used[1] else s_dot, before + used[2] + 1)
                    elif not sample:
                        pool.wait_ge(s_vsum, before - RING + place + 1)
                    pool.sem_inc(s_pool_turn, 1)
                    pool.indirect_dma_start(
                        out=ring[:, place % RING, :], out_offset=None, in_=peer_v if is_v else peer_u,
                        in_offset=bass.IndirectOffsetOnAxis(ap=idx[:, e:e + 1], axis=0)).then_inc(s_row[place % RING], 16)

            gathers(0, True)
            with pool.Fori(0, BLOCKS - 1) as i:
                gathers(i + 1, False)
            gathers(BLOCKS, False)

        @block.tensor
        def _(pe):
            def mm(out, lhsT, rhs, start=True, stop=True):
                return nc.tensor.matmul(out, lhsT, rhs, start=start, stop=stop)

            def project(out, lo, width, n):
                for c in range(CM):
                    last = mm(out, win[:, c, lo:lo + width], xT[:, c, 0:n], start=c == 0, stop=c == CM - 1)
                return last

            def mixer(v, w, n, full, tick):
                prompt = n == P
                if tick == T_XT:
                    if not is_count(v, 0):
                        pe.wait_ge(s_lru, v)
                        pe.wait_ge(s_c, v)
                        pe.wait_ge(s_topk, (w if full else 1) * PEER_HEADS)
                    else:
                        pe.wait_ge(s_const, 7)
                    pe.wait_ge(s_xn, v + 1)
                    for c in range(CM):
                        last = nc.tensor.transpose(by4(bank[c // 4])[:, c % 4, 0:n], xn[0:n, c * P:(c + 1) * P], ident[0:n, 0:n])
                    last.then_inc(s_xt_ps, 1)
                if T_XL <= tick < T_XL + FT:
                    f = tick - T_XL
                    if f == 0:
                        pe.wait_ge(s_win[0], 16)
                        pe.wait_ge(s_xt, v + 1)
                    last = project(by4(bC)[:, f, 0:n], P * f, P, n)
                    if f == FT - 1:
                        last.then_inc(s_xl_ps, 1)
                if tick == T_GATES:
                    pe.wait_ge(s_win[6], 16)
                    project(bB[0:HEADS, 0:n], D_IN - 2 * HEADS, HEADS, n)
                    project(bB[0:HEADS, P:P + n], D_IN - HEADS, HEADS, n).then_inc(s_g_ps, 1)
                if full and tick in (T_GL, T_GL + 1, T_GL + 3, T_GL + 4):
                    f = (T_GL, T_GL + 1, T_GL + 3, T_GL + 4).index(tick)
                    if f == 0:
                        pe.wait_ge(s_win[1], 16)
                    last = project(by4(bD)[:, f, 0:n], 512 + P * f, P, n)
                    if f == FT - 1:
                        last.then_inc(s_gl_ps, 1)
                if full and tick in (T_Q, T_Q + 1, T_Q + 3, T_Q + 4):
                    f = (T_Q, T_Q + 1, T_Q + 3, T_Q + 4).index(tick)
                    if f == 0:
                        pe.wait_ge(s_win[2], 16)
                    last = project(by4(bE)[:, f, 0:n], 1024 + P * f, P, n)
                    if f == FT - 1:
                        last.then_inc(s_q_ps, 1)
                if tick in (T_K, T_K + 1, T_K + 3, T_K + 4):
                    f = (T_K, T_K + 1, T_K + 3, T_K + 4).index(tick)
                    if f == 0:
                        pe.wait_ge(s_win[3], 16)
                    last = project(by4(bF)[:, f, 0:n], 1536 + P * f, P, n)
                    if f == FT - 1:
                        last.then_inc(s_k_ps, 1)
                if tick == T_LRU + 4:
                    if is_count(v, 0):
                        pe.wait_ge(s_blocks, 64)
                    pe.wait_ge(s_xc, v + 1)
                    pe.wait_ge(s_xl, v + 1)
                    if full:
                        pe.wait_ge(s_q, w + 1)
                    for f in range(FT):
                        mm(by4(bC)[:, f, 0:n], wa[:, f, :], xc[:, f, 0:n])
                    for f in range(FT):
                        last = mm(by4(bE)[:, f, 0:n], wx[:, f, :], xc[:, f, 0:n])
                    last.then_inc(s_ri_ps, 1)
                if tick in (T_V, T_V + 1, T_V + 3, T_V + 4):
                    part = (T_V, T_V + 1, T_V + 3, T_V + 4).index(tick)
                    if part == 0:
                        pe.wait_ge(s_win[4], 16)
                    for c in (2 * part, 2 * part + 1):
                        last = mm(bA[0:n, :], xT[:, c, 0:n], win[:, c, 2048:2560], start=c == 0, stop=c == CM - 1)
                    if part == 3:
                        last.then_inc(s_v_ps, 1)
                if tick == T_V + 5:
                    pe.wait_ge(s_k, v + 1)
                    for f in range(HEADS):
                        last = nc.tensor.transpose(by4(bF)[0:n, f, :], kT[:, f, 0:n], ident[:, :])
                    last.then_inc(s_kt_ps, 1)
                if tick == T_V + 6:
                    if full:
                        pe.wait_ge(s_gl, w + 1)
                    pe.wait_ge(s_rows, v + 1)
                    pe.wait_ge(s_dg, v + 1)
                    for a, r in enumerate((3, 1, 2)):
                        mm(bD[0:n, HEADS * a:HEADS * a + HEADS], rows[r][:, 0:n], ident[0:HEADS, 0:HEADS])
                    mm(bD[:, 16:20], ones4[:, :], dg4[:, :]).then_inc(s_cols_ps, 1)
                if full and tick in (T_O, T_O + 1, T_O + 3, T_O + 4):
                    part = (T_O, T_O + 1, T_O + 3, T_O + 4).index(tick)
                    if part == 0:
                        pe.wait_ge(s_win[5], 16)
                        pe.wait_ge(s_ri_exp, v + 1)
                    for c in (2 * part, 2 * part + 1):
                        last = mm(bE[0:n, :], xT[:, c, 0:n], win[:, c, 2560:3072], start=c == 0, stop=c == CM - 1)
                    if part == 3:
                        last.then_inc(s_o_ps, 1)
                if full and tick == T_CHUNK - 2:
                    pe.wait_ge(s_v, v + 1)
                    for f in range(HEADS):
                        sel = spread(ident[0:HEADS, f:f + 1], 1, P)
                        mm(by4(bA)[:, f, 0:n], sel, rows[5][:, 0:n])
                        last = mm(by4(bB)[:, f, 0:n], sel, rows[4][:, 0:n])
                    last.then_inc(s_bc_ps, 1)
                if full and tick == T_CHUNK + 2:
                    pe.wait_ge(s_lru, v + 1)
                    for f in range(HEADS):
                        last = mm(by4(bC)[0:n, f, 0:n], kT[:, f, 0:n], qT[:, f, 0:n])
                    last.then_inc(s_s_ps, 1)
                if full and tick == T_CHUNK + 7:
                    pe.wait_ge(s_qd, w + 1)
                    pe.wait_ge(s_p, w + 1)
                    for f in range(HEADS):
                        out = pair(bank[f // 2])[0:n, f % 2, :]
                        mm(out, t3[0:n, f, 0:n], vt[0:n, f, :], stop=False)
                        last = mm(out, t2[:, f, 0:n], C[:, f, :], start=False)
                    last.then_inc(s_num_ps, 1)
                if tick == T_CHUNK + 8:
                    pe.wait_ge(s_kw, v + 1)
                    pe.wait_ge(s_cols, v + 1)
                    pe.wait_ge(s_v, v + 1)
                    pe.wait_ge(s_lru, v + 1)
                    for f in range(HEADS):
                        last = mm(pair(bank[2 + f // 2])[:, f % 2, :], kw[0:n, f, :], vt[0:n, f, :])
                    last.then_inc(s_c_ps, 1)
                if not full:
                    return
                if tick == T_OUT - 3:
                    pe.wait_ge(s_ym, w + 1)
                    for f in range(HEADS):
                        last = nc.tensor.transpose(by4(bF)[:, f, 0:n], t1[0:n, f, :], ident[0:n, 0:n])
                    last.then_inc(s_ym_ps, 1)
                if T_OUT <= tick < T_OUT + CM:
                    c = tick - T_OUT
                    if c == 0:
                        pe.wait_ge(s_wout, 16)
                        pe.wait_ge(s_ymT, w + 1)
                        pe.wait_ge(s_num, w + 1)
                        pe.wait_ge(s_lru, v + 1)
                    y = G[:, c, 0:n] if c < FT else xc[:, c - FT, 0:n]
                    for half in range(2):
                        last = mm(bank[half][0:n, :], y, wout[:, c, 512 * half:512 * half + 512], start=c == 0, stop=c == CM - 1)
                    if c == CM - 1:
                        last.then_inc(s_out_ps, 1)
                if tick == T_NORM2 + 4:
                    pe.wait_ge(s_xn2, w + 1)
                    pe.wait_ge(s_c, v + 1)
                    for c in range(CM):
                        last = nc.tensor.transpose(by4(bank[2 + c // 4])[:, c % 4, 0:n], xn[0:n, c * P:(c + 1) * P], ident[0:n, 0:n])
                    last.then_inc(s_x2_ps, 1)
                for ft in range(2 * PEER_HEADS):
                    at = T_QUERY + TOPK_TICKS * (ft // 2) + 2 * (ft % 2)
                    if tick == at:
                        out = bank[4 + ft % 2][:, 0:n]
                        if ft == 0:
                            pe.wait_ge(s_x2, w + 1)
                        if ft >= 2:
                            pe.wait_ge(s_q2, w * 16 + ft - 1)
                        pe.wait_ge(s_wq[ft % 2], w * 128 + 16 * (ft // 2) + 16)
                        for c in range(CM):
                            last = mm(out, wq_buf[ft % 2][:, c, :], xT[:, c, 0:n], start=c == 0, stop=c == CM - 1)
                        last.then_inc(s_qp_ps, 1)
                    if tick == at + 1:
                        hh = ft // 2
                        if ft % 2 == 0 and hh >= 2:
                            pe.wait_ge(s_topk, w * PEER_HEADS + hh - 1)
                        pe.wait_ge(s_q2, w * 16 + ft + 1)
                        mm(bank[2 * (hh % 2) + ft % 2][0:n, 0:P], q2[:, ft % 2, 0:n], keysT[:, ft % 2, :]).then_inc(s_score, 1)

            def take_up(w, sample):
                n = SAMPLE if sample else P
                pe.wait_ge(s_h2, w + 1)
                if not sample:
                    pe.wait_ge(s_acc_out, w)
                for half in range(2):
                    last = mm(acc[0:n, 512 * half:512 * half + 512], ident[0:n, 0:n], h[0:n, 512 * half:512 * half + 512], stop=False)
                last.then_inc(s_acc0, 1)

            def expert(w, sample, tick):
                j = tick - TOPK
                if not 0 <= j < n_experts(sample):
                    return
                place = v_place(j, sample)
                pe.wait_ge(s_row[place % RING], (gathers_before(w, sample) + place // RING + 1) * 16)
                pe.wait_ge(s_diag, experts_before(w, sample) + j + 1)
                n = SAMPLE if sample else P
                for half in range(2):
                    last = mm(acc[0:n, 512 * half:512 * half + 512], diag[:, j % DIAGS, 0:n],
                              ring[:, place % RING, 512 * half:512 * half + 512], start=False, stop=j == n_experts(sample) - 1)
                last.then_inc(s_vsum, 1)

            for tick in range(TICKS):
                mixer(0, 0, SAMPLE, True, tick)
            take_up(0, True)
            for tick in range(TICKS):
                mixer(1, 1, META, False, tick)
            for tick in range(SAMPLE + TOPK):
                expert(0, True, tick)
                for t in range(3 * tick, 3 * tick + 3):
                    mixer(2, 1, P, True, t)
            with pe.Fori(0, BLOCKS - 1) as i:
                take_up(i + 1, False)
                for tick in range(TICKS):
                    expert(i + 1, False, tick)
                    mixer(i + 3, i + 2, P, True, tick)
            take_up(BLOCKS, False)
            for tick in range(TICKS):
                expert(BLOCKS, False, tick)

        @block.scalar
        def _(act):
            count = [0]

            def link(ins):
                count[0] += 1
                ins.then_inc(s_act, 1)
                act.wait_ge(s_act, count[0])

            def restart():
                act.sem_clear(s_act)
                count[0] = 0

            def a(out, in_, func, **kw):
                return nc.scalar.activation(out, in_, func, **kw)

            def rstd(n, col, width):
                link(a(stat[0:n, col + 1:col + 2], stat[0:n, col:col + 1], ACT.Ln, scale=1.0 / width, bias=eps[0:n, :]))
                return a(stat[0:n, col + 2:col + 3], stat[0:n, col + 1:col + 2], ACT.Exp, scale=-0.5)

            def mixer(v, w, n, full, tick):
                if tick == T_NORM:
                    act.wait_ge(s_x, 16 * v + 16)
                    if not is_count(v, 0):
                        act.wait_ge(s_xcur, w if full else 1)
                        act.wait_ge(s_lru, v)
                    link(a(xn[0:n, :], h[0:n, :], ACT.Square, accum_out=stat[0:n, 0:1]))
                    link(rstd(n, 0, D_MODEL))
                    a(xn[0:n, :], h[0:n, :], ACT.Copy, scale=stat[0:n, 2:3]).then_inc(s_xn, 1)
                if tick == T_XT_OUT:
                    act.wait_ge(s_small, 96)
                    act.wait_ge(s_xt_ps, v + 1)
                    if full and not is_count(w, 0) and not is_count(w, 1):
                        act.wait_ge(s_y_out, w * 16 - 16)
                    for c in range(CM):
                        last = a(xT[:, c, 0:n], by4(bank[c // 4])[:, c % 4, 0:n], ACT.Copy, scale=vec[:, nmix][:, c:c + 1])
                    last.then_inc(s_xt, 1)
                if tick == T_XL + FT:
                    if is_count(v, 0):
                        act.wait_ge(s_state_in, 64)
                    if is_count(v, 1):
                        act.wait_ge(s_reset, 1)
                    act.wait_ge(s_xl_ps, v + 1)
                    a(xl[:, :, CONV_W - 1:CONV_W - 1 + n], by4(bC)[:, :, 0:n], ACT.Copy).then_inc(s_xl, 1)
                if tick == T_ROWS - 1:
                    act.wait_ge(s_g_ps, v + 1)
                    if not is_count(w, 0):
                        act.wait_ge(s_sel, w)
                    act.wait_ge(s_setup, 1)
                    a(rows[0][:, 0:n], bB[0:HEADS, P:P + n], ACT.Identity, scale=-1.0, bias=nbf[:, :]).then_inc(s_fneg, 1)
                if tick == T_ROWS + 1:
                    act.wait_ge(s_fabs, v + 1)
                    link(a(rows[1][:, 0:n], rows[1][:, 0:n], ACT.Exp, scale=-1.0))
                    a(rows[1][:, 0:n], rows[1][:, 0:n], ACT.Ln, bias=1.0).then_inc(s_fln, 1)
                if full and tick == T_GL + 5:
                    act.wait_ge(s_gl_ps, w + 1)
                    a(G[:, :, 0:n], by4(bD)[:, :, 0:n], ACT.Copy)
                    a(t3[:, :, 0:n], by4(bD)[:, :, 0:n], ACT.Square).then_inc(s_gl, 1)
                if full and tick == T_GL + 7:
                    act.wait_ge(s_gl_arg, w + 1)
                    a(t3[:, :, 0:n], t3[:, :, 0:n], ACT.Exp, scale=GELU_SCALE).then_inc(s_gl_exp, 1)
                if tick == T_ROWS + 4:
                    act.wait_ge(s_mrow, v + 1)
                    a(rows[1][:, 0:n], rows[0][:, 0:n], ACT.Exp, scale=-1.0)
                    a(rows[2][:, 0:n], rows[3][:, 0:n], ACT.Exp, bias=rows[5][:, n - 1:n])
                    a(rows[4][:, 0:n], rows[4][:, 0:n], ACT.Exp, scale=-1.0, bias=mst[:, :]).then_inc(s_rows, 1)
                if full and tick == T_Q + 5:
                    act.wait_ge(s_q_ps, w + 1)
                    a(qT[:, :, 0:n], by4(bE)[:, :, 0:n], ACT.Copy).then_inc(s_q, 1)
                if tick == T_K + 5:
                    act.wait_ge(s_k_ps, v + 1)
                    a(kT[:, :, 0:n], by4(bF)[:, :, 0:n], ACT.Copy, scale=float(HEAD) ** -0.5).then_inc(s_k, 1)
                if tick == T_LRU + 5:
                    act.wait_ge(s_ri_ps, v + 1)
                    for f in range(FT):
                        a(t1[:, f, 0:n], by4(bC)[:, f, 0:n], ACT.Exp, scale=-1.0, bias=neg[:, f:f + 1])
                    for f in range(FT):
                        last = a(t2[:, f, 0:n], by4(bE)[:, f, 0:n], ACT.Exp, scale=-1.0, bias=neg[:, FT + f:FT + f + 1])
                    last.then_inc(s_ri_exp, 1)
                if tick == T_LRU + 7:
                    act.wait_ge(s_r, v + 1)
                    for f in range(FT):
                        last = a(t3[:, f, 0:n], t1[:, f, 0:n], ACT.Exp, scale=decay_c[:, f:f + 1])
                    last.then_inc(s_a, 1)
                if tick == T_V + 5:
                    act.wait_ge(s_v_ps, v + 1)
                    a(vt[0:n, :, 0:HEAD], by4(bA)[0:n, :, :], ACT.Copy).then_inc(s_v, 1)
                if tick == T_LRU + 12:
                    act.wait_ge(s_m2, v + 1)
                    link(a(t1[:, :, 0:n], t1[:, :, 0:n], ACT.Ln))
                    a(t1[:, :, 0:n], t1[:, :, 0:n], ACT.Exp, scale=0.5).then_inc(s_mult, 1)
                if tick == T_V + 7:
                    act.wait_ge(s_cols_ps, v + 1)
                    a(cols[0:n, 0:3, :], bD[0:n, 0:12].rearrange("p (a h) -> p a h", a=3), ACT.Copy)
                    a(cols[:, 4, :], bD[:, 16:20], ACT.Copy).then_inc(s_cols, 1)
                if full and tick == T_CHUNK:
                    act.wait_ge(s_wmask, w + 1)
                    act.wait_ge(s_cols, v + 1)
                    for f in range(HEADS):
                        last = a(t3[0:n, f, 0:n], t3[0:n, f, 0:n], ACT.Exp, bias=cols[0:n, 0, f:f + 1])
                    last.then_inc(s_w, 1)
                if full and tick == T_CHUNK + 8:
                    act.wait_ge(s_o_ps, w + 1)
                    act.wait_ge(s_num_ps, w + 1)
                    a(sigo[0:n, :, :], by4(bE)[0:n, :, :], ACT.Exp, scale=-1.0).then_inc(s_o, 1)
                if full and tick == T_CHUNK + 12:
                    act.wait_ge(s_hsq, w + 1)
                    link(a(hstat[0:n, :], hstat[0:n, :], ACT.Ln, scale=1.0 / HEAD, bias=eps[0:n, :]))
                    a(hstat[0:n, :], hstat[0:n, :], ACT.Exp, scale=-0.5).then_inc(s_hrs, 1)
                if full and tick == T_OUT - 1:
                    act.wait_ge(s_ym_ps, w + 1)
                    for f in range(HEADS):
                        last = a(xc[:, f, 0:n], by4(bF)[:, f, 0:n], ACT.Copy, scale=vec[:, mnorm][:, f:f + 1])
                    last.then_inc(s_ymT, 1)
                if full and tick == T_NORM2 + 1:
                    act.wait_ge(s_h2, w + 1)
                    link(a(xn[0:n, :], h[0:n, :], ACT.Square, accum_out=stat[0:n, 3:4]))
                    rstd(n, 3, D_MODEL).then_inc(s_rstd2, 1)
                if full and tick == T_NORM2 + 5:
                    act.wait_ge(s_x2_ps, w + 1)
                    a(xT[:, 0:4, 0:n], by4(bC)[:, :, 0:n], ACT.Copy)
                    a(xT[:, 4:8, 0:n], by4(bD)[:, :, 0:n], ACT.Copy).then_inc(s_x2, 1)
                if full:
                    for ft in range(2 * PEER_HEADS):
                        if tick == T_QUERY + TOPK_TICKS * (ft // 2) + 2 * (ft % 2) + 1:
                            act.wait_ge(s_qp_ps, w * 16 + ft + 1)
                            if ft >= 2:
                                act.wait_ge(s_score, w * 16 + ft - 1)
                            a(q2[:, ft % 2, 0:n], bank[4 + ft % 2][:, 0:n], ACT.Copy).then_inc(s_q2, 1)
                if full and tick == T_TOPK + TOPK_TICKS * PEER_HEADS + 1:
                    act.wait_ge(s_shift, w + 1)
                    a(gate_n[0:n, :, :], gate_n[0:n, :, :], ACT.Exp).then_inc(s_gate_e, 1)

            def take_over(w, sample):
                act.wait_ge(s_x2, w + 1)
                if sample:
                    for q in range(COPIES):
                        last = a(xcur[SAMPLE * q:SAMPLE * q + SAMPLE, :], xn[0:SAMPLE, :], ACT.Copy)
                else:
                    act.wait_ge(s_dot, experts_before(w, sample))
                    last = a(xcur[:, :], xn[:, :], ACT.Copy)
                last.then_inc(s_xcur, 1)

            def expert(w, sample, tick):
                j = tick - TOPK
                n = SAMPLE if sample else P
                before = experts_before(w, sample)
                if tick and tick % TOPK == 0 and tick <= n_experts(sample):
                    act.wait_ge(s_arg, groups_before(w, sample) + tick // TOPK)
                    a(gl_a[:, :], gl_a[:, :], ACT.Exp, scale=GELU_SCALE).then_inc(s_gexp, 1)
                if not 0 <= j < n_experts(sample):
                    return
                if j % TOPK == 0:
                    act.wait_ge(s_coef, groups_before(w, sample) + j // TOPK + 1)
                if j >= DIAGS or not sample:
                    act.wait_ge(s_vsum, before + j - DIAGS + 1)
                a(diag[:, j % DIAGS, 0:n], rep[:, :] if sample else ident[:, :], ACT.Copy,
                  scale=coef[:, j:j + 1]).then_inc(s_diag, 1)

            def finish(w, sample):
                n = SAMPLE if sample else P
                act.wait_ge(s_vsum, experts_before(w, sample) + n_experts(sample))
                rowsT = xT[0:n, :, :].rearrange("p c t -> p (c t)")
                if not sample:
                    act.wait_ge(s_y_out, w * 16)
                link(a(rowsT, acc[0:n, :], ACT.Square, accum_out=stat[0:n, 6:7]))
                a(rowsT, acc[0:n, :], ACT.Copy).then_inc(s_acc_out, 1)
                rstd(n, 6, D_MODEL).then_inc(s_rstd_y, 1)

            nc.scalar.preload_act_table_set("natural_log_exp_and_others")
            act.wait_ge(s_const, 7)
            act.wait_ge(s_setup_a, 1)
            a(sp_t[:, 1, :], sp_t[:, 1, :], ACT.Exp, scale=-1.0).then_inc(s_setup_e, 1)
            act.wait_ge(s_setup_e, 1)
            a(sp_t[:, 2, :], sp_t[:, 1, :], ACT.Ln, bias=1.0).then_inc(s_setup_l, 1)
            for tick in range(TICKS):
                mixer(0, 0, SAMPLE, True, tick)
            take_over(0, True)
            for tick in range(TICKS):
                mixer(1, 1, META, False, tick)
            for tick in range(SAMPLE + TOPK):
                expert(0, True, tick)
                for t in range(3 * tick, 3 * tick + 3):
                    mixer(2, 1, P, True, t)
            finish(0, True)
            with act.Fori(0, BLOCKS - 1) as i:
                restart()
                take_over(i + 1, False)
                for tick in range(TICKS):
                    expert(i + 1, False, tick)
                    mixer(i + 3, i + 2, P, True, tick)
                finish(i + 1, False)
            restart()
            take_over(BLOCKS, False)
            for tick in range(TICKS):
                expert(BLOCKS, False, tick)
            finish(BLOCKS, False)

        @block.vector
        def _(dve):
            count = [0]

            def link(ins):
                count[0] += 1
                ins.then_inc(s_dve, 1)
                dve.wait_ge(s_dve, count[0])
                return ins

            def held():
                dve.sem_inc(s_dve_turn, 1)

            def restart():
                dve.sem_clear(s_dve)
                count[0] = 0

            tt, ts, stt = dve.tensor_tensor, dve.tensor_scalar, dve.scalar_tensor_tensor

            def setup():
                dve.wait_ge(s_small, 96)
                link(ts(sp_t[:, 0, :], vec[:, lam], -1.0, None, ALU.mult))
                stt(sp_t[:, 1, :], sp_t[:, 0, :], -1.0, sp_t[:, 0, :], ALU.mult, ALU.max).then_inc(s_setup_a, 1)
                ts(neg[:, :], vec[:, 0:2 * FT], -1.0, None, ALU.mult)
                ts(nbf[:, :], bg[:, 1:2], -1.0, None, ALU.mult)
                dve.wait_ge(s_setup_l, 1)
                e, ln, z, z2, p = (sp_t[:, k, :] for k in (1, 2, 3, 4, 5))
                link(ts(z, e, 2.0, None, ALU.add))
                link(dve.reciprocal(z, z))
                link(tt(z, z, e, ALU.mult))
                link(tt(z2, z, z, ALU.mult))
                link(ts(p, z2, 1.0 / 7, 1.0 / 5, ALU.mult, ALU.add))
                link(tt(p, p, z2, ALU.mult))
                link(ts(p, p, 1.0 / 3, None, ALU.add))
                link(tt(p, p, z2, ALU.mult))
                link(ts(p, p, 1.0, 2.0, ALU.add, ALU.mult))
                link(tt(p, p, z, ALU.mult))
                link(ts(z2.bitcast(u32), e, 0.2, None, ALU.is_lt))
                link(dve.copy_predicated(ln, z2.bitcast(u32), p))
                link(stt(ln, sp_t[:, 0, :], 0.0, ln, ALU.max, ALU.add))
                ts(decay_c[:, 0:FT], ln, -8.0, None, ALU.mult)
                ts(decay_c[:, FT:2 * FT], ln, 16.0, None, ALU.mult).then_inc(s_setup, 1)

            def top16(values, work, out_v, out_i, n):
                link(dve.max(out_v[:, 0:8], values))
                link(dve.match_replace(work, out_v[:, 0:8], values, -3.0e38))
                link(dve.max(out_v[:, 8:16], work))
                dve.max_index(out_i[:, 0:8], out_v[:, 0:8], values)
                return link(dve.max_index(out_i[:, 8:16], out_v[:, 8:16], work))

            def pick(hh, which, n):
                oh = tk_s[0:n, :].rearrange("p (k j) -> p k j", k=TOPK)
                link(tt(oh, spread(ci[0:n, 1 + which, :].unsqueeze(2), 2, TOPK),
                        spread(iota[0:n, :].unsqueeze(1), 1, TOPK), ALU.is_equal))
                link(tt(oh, oh, spread(topi[0:n, which, :].unsqueeze(1), 1, TOPK), ALU.mult))
                link(dve.tensor_reduce(eh[0:n, which, :], oh, AX.X, ALU.add))

            def topk(w, n, hh, step):
                src = bank[2 * (hh % 2) + min(step, 1)]
                if step == 0:
                    if hh == 0 and not is_count(w, 0):
                        dve.wait_ge(s_idx_cur, 2 * w)
                    dve.wait_ge(s_score, w * 16 + 2 * hh + 1)
                    held()
                    top16(src[0:n, 0:P], tk_s[0:n, 0:P], tops[0:n, 0, :], topi[0:n, 0, :], n)
                if step == 1:
                    dve.wait_ge(s_score, w * 16 + 2 * hh + 2)
                    held()
                    top16(src[0:n, 0:P], tk_s[0:n, P:2 * P], tops[0:n, 1, :], topi[0:n, 1, :], n)
                    cand = tk_c[0:n, :].rearrange("p (a b) -> p a b", a=TOPK)
                    tt(cand, spread(tops[0:n, 0, :].unsqueeze(2), 2, TOPK),
                       spread(tops[0:n, 1, :].unsqueeze(1), 1, TOPK), ALU.add).then_inc(s_topk, 1)
                if step == 2:
                    dve.wait_ge(s_topk, w * PEER_HEADS + hh + 1)
                    held()
                    top16(tk_c[0:n, :], tk_s[0:n, :], gate_n[0:n, hh, :], ci[0:n, 0, :], n)
                if step == 3:
                    ts(ci[0:n, 1, :], ci[0:n, 0, :], 4, None, ALU.logical_shift_right)
                    link(ts(ci[0:n, 2, :], ci[0:n, 0, :], TOPK - 1, None, ALU.bitwise_and))
                    pick(hh, 0, n)
                if step == 4:
                    pick(hh, 1, n)
                    link(stt(idx_n[0:n, TOPK * hh:TOPK * hh + TOPK], eh[0:n, 0, :], float(P), eh[0:n, 1, :], ALU.mult, ALU.add))

            def mixer(v, w, n, full, tick):
                if tick == T_CONV:
                    dve.wait_ge(s_xl, v + 1)
                    for j in range(CONV_W):
                        for f in range(FT):
                            src = xl[:, f, j:j + n]
                            if j == 0:
                                last = ts(xc[:, f, 0:n], src, cw[:, f, 0:1], vec[:, convb][:, f:f + 1], ALU.mult, ALU.add)
                            else:
                                last = stt(xc[:, f, 0:n], src, cw[:, f, j:j + 1], xc[:, f, 0:n], ALU.mult, ALU.add)
                        if j < CONV_W - 1:
                            link(last)
                        else:
                            last.then_inc(s_xc, 1)
                    dve.wait_ge(s_xc, v + 1)
                    link(dve.tensor_copy(xl[:, :, 0:CONV_W - 1], xl[:, :, n:n + CONV_W - 1]))
                if tick == T_ROWS:
                    dve.wait_ge(s_fneg, v + 1)
                    stt(rows[1][:, 0:n], rows[0][:, 0:n], -1.0, rows[0][:, 0:n], ALU.mult, ALU.max).then_inc(s_fabs, 1)
                if tick == T_ROWS + 3:
                    dve.wait_ge(s_fln, v + 1)
                    link(stt(rows[1][:, 0:n], rows[0][:, 0:n], 0.0, rows[1][:, 0:n], ALU.max, ALU.add))
                    link(dve.tensor_tensor_scan(rows[2][:, 0:n], ones4[:, 0:n], rows[1][:, 0:n], 0.0, ALU.mult, ALU.subtract))
                    link(stt(rows[3][:, 0:n], bB[0:HEADS, 0:n], bg[:, 0:1], rows[2][:, 0:n], ALU.add, ALU.subtract))
                    link(dve.tensor_tensor_scan(rows[4][:, 0:n], rows[3][:, 0:n], rows[3][:, 0:n], mst[:, :], ALU.max, ALU.max))
                    ts(rows[5][:, 0:n], rows[4][:, 0:n], -1.0, None, ALU.mult)
                    tt(rows[0][:, 0:n], rows[2][:, 0:n], rows[4][:, 0:n], ALU.add).then_inc(s_mrow, 1)
                if full and tick == T_GL + 6:
                    dve.wait_ge(s_gl, w + 1)
                    link(ts(t3[:, :, 0:n], t3[:, :, 0:n], GELU_CUBIC, 1.0, ALU.mult, ALU.add))
                    link(tt(t3[:, :, 0:n], t3[:, :, 0:n], G[:, :, 0:n], ALU.mult))
                    ts(t3[:, :, 0:n], t3[:, :, 0:n], -50.0, None, ALU.max).then_inc(s_gl_arg, 1)
                if full and tick == T_GL + 8:
                    dve.wait_ge(s_gl_exp, w + 1)
                    link(ts(t3[:, :, 0:n], t3[:, :, 0:n], 1.0, None, ALU.add))
                    link(dve.reciprocal(t3[:, :, 0:n], t3[:, :, 0:n]))
                    link(tt(G[:, :, 0:n], G[:, :, 0:n], t3[:, :, 0:n], ALU.mult))
                if tick == T_ROWS + 6:
                    dve.wait_ge(s_rows, v + 1)
                    link(dve.tensor_copy(mst[:, :], rows[0][:, n - 1:n]))
                    ts(dg4[:, :], ident[0:HEADS, 0:HEADS], rows[4][:, n - 1:n], None, ALU.mult).then_inc(s_dg, 1)
                if tick == T_LRU + 6:
                    dve.wait_ge(s_ri_exp, v + 1)
                    link(ts(t1[:, :, 0:n], t1[:, :, 0:n], 1.0, None, ALU.add))
                    dve.reciprocal(t1[:, :, 0:n], t1[:, :, 0:n]).then_inc(s_r, 1)
                    link(ts(t2[:, :, 0:n], t2[:, :, 0:n], 1.0, None, ALU.add))
                if tick == T_LRU + 7:
                    link(dve.reciprocal(t2[:, :, 0:n], t2[:, :, 0:n]))
                    dve.wait_ge(s_r, v + 1)
                    link(tt(t4[:, :, 0:n], t1[:, :, 0:n], spread(decay_c[:, FT:2 * FT].unsqueeze(2), 2, n), ALU.mult))
                    tt(t2[:, :, 0:n], t2[:, :, 0:n], xc[:, :, 0:n], ALU.mult)
                    link(ts(by4(bC)[:, :, 0:n], t4[:, :, 0:n], 1.0 / 120, None, ALU.mult))
                if tick == T_LRU + 8:
                    for c in (-1.0 / 24, 1.0 / 6):
                        link(stt(by4(bC)[:, :, 0:n], by4(bC)[:, :, 0:n], c, t4[:, :, 0:n], ALU.add, ALU.mult))
                if tick == T_LRU + 9:
                    for c in (-0.5, 1.0):
                        link(stt(by4(bC)[:, :, 0:n], by4(bC)[:, :, 0:n], c, t4[:, :, 0:n], ALU.add, ALU.mult))
                    link(ts(t4[:, :, 0:n].bitcast(u32), t4[:, :, 0:n], 0.125, None, ALU.is_lt))
                if tick == T_LRU + 10:
                    dve.wait_ge(s_a, v + 1)
                    link(tt(t1[:, :, 0:n], t3[:, :, 0:n], t3[:, :, 0:n], ALU.mult))
                    link(ts(t1[:, :, 0:n], t1[:, :, 0:n], -1.0, 1.0, ALU.mult, ALU.add))
                    link(dve.copy_predicated(t1[:, :, 0:n], t4[:, :, 0:n].bitcast(u32), by4(bC)[:, :, 0:n]))
                    ts(t1[:, :, 0:n], t1[:, :, 0:n], 2.0 ** -60, None, ALU.max).then_inc(s_m2, 1)
                if tick == T_LRU + 13:
                    dve.wait_ge(s_mult, v + 1)
                    if is_count(v, 1):
                        link(dve.memset(t1[:, :, 0:1], 1.0))
                    link(tt(t2[:, :, 0:n], t2[:, :, 0:n], t1[:, :, 0:n], ALU.mult))
                    for f in range(FT):
                        last = dve.tensor_tensor_scan(t4[:, f, 0:n], t3[:, f, 0:n], t2[:, f, 0:n], hst[:, f:f + 1], ALU.mult, ALU.add)
                    link(last)
                if tick == T_LRU + 14:
                    last = dve.tensor_copy(hst[:, :].unsqueeze(2), t4[:, :, n - 1:n])
                    if full:
                        last = tt(G[:, :, 0:n], G[:, :, 0:n], t4[:, :, 0:n], ALU.mult)
                    last.then_inc(s_lru, 1)
                if tick == T_V + 8:
                    dve.wait_ge(s_kt_ps, v + 1)
                    dve.wait_ge(s_cols, v + 1)
                    tt(kw[0:n, :, :], by4(bF)[0:n, :, :], spread(cols[0:n, 2, :].unsqueeze(2), 2, HEAD), ALU.mult).then_inc(s_kw, 1)
                if full and tick == T_CHUNK - 1:
                    dve.wait_ge(s_bc_ps, w + 1)
                    tt(t3[0:n, :, 0:n], by4(bA)[0:n, :, 0:n], spread(mask[0:n, 0:n].unsqueeze(1), 1, HEADS), ALU.add).then_inc(s_wmask, 1)
                    dve.wait_ge(s_q, w + 1)
                    tt(t2[:, :, 0:n], by4(bB)[:, :, 0:n], qT[:, :, 0:n], ALU.mult).then_inc(s_qd, 1)
                if full and tick == T_CHUNK + 4:
                    dve.wait_ge(s_w, w + 1)
                    dve.wait_ge(s_s_ps, w + 1)
                    tt(t3[0:n, :, 0:n], t3[0:n, :, 0:n], by4(bC)[0:n, :, 0:n], ALU.mult).then_inc(s_p, 1)
                if full and tick == T_CHUNK + 9:
                    dve.wait_ge(s_num_ps, w + 1)
                    for b in range(2):
                        last = dve.tensor_copy(den[0:n, 2 * b:2 * b + 2].unsqueeze(2), pair(bank[b])[0:n, :, HEAD:HEAD + 1])
                    link(last)
                    link(stt(den[0:n, :], den[0:n, :], -1.0, den[0:n, :], ALU.mult, ALU.max))
                    link(tt(den[0:n, :], den[0:n, :], cols[0:n, 1, :], ALU.max))
                    link(dve.reciprocal(den[0:n, :], den[0:n, :]))
                    for b in range(2):
                        last = tt(t1[0:n, 2 * b:2 * b + 2, :], pair(bank[b])[0:n, :, 0:HEAD],
                                  spread(den[0:n, 2 * b:2 * b + 2].unsqueeze(2), 2, HEAD), ALU.mult)
                    last.then_inc(s_num, 1)
                if full and tick == T_CHUNK + 10:
                    dve.wait_ge(s_num, w + 1)
                    link(tt(t4[0:n, :, :], t1[0:n, :, :], t1[0:n, :, :], ALU.mult))
                    dve.tensor_reduce(hstat[0:n, :], t4[0:n, :, :], AX.X, ALU.add).then_inc(s_hsq, 1)
                if tick == T_CHUNK + 11:
                    dve.wait_ge(s_c_ps, v + 1)
                    for f in range(HEADS):
                        last = stt(C[:, f, :], C[:, f, :], cols[:, 4, f:f + 1], pair(bank[2 + f // 2])[:, f % 2, :], ALU.mult, ALU.add)
                    last.then_inc(s_c, 1)
                if not full:
                    return
                if tick == T_CHUNK + 13:
                    dve.wait_ge(s_o, w + 1)
                    link(ts(sigo[0:n, :, :], sigo[0:n, :, :], 1.0, None, ALU.add))
                    link(dve.reciprocal(sigo[0:n, :, :], sigo[0:n, :, :]))
                if tick == T_CHUNK + 14:
                    link(tt(t1[0:n, :, :], t1[0:n, :, :], sigo[0:n, :, :], ALU.mult))
                    dve.wait_ge(s_hrs, w + 1)
                    tt(t1[0:n, :, :], t1[0:n, :, :], spread(hstat[0:n, :].unsqueeze(2), 2, HEAD), ALU.mult).then_inc(s_ym, 1)
                if tick == T_NORM2 - 1:
                    dve.wait_ge(s_out_ps, w + 1)
                    for half in range(2):
                        last = tt(h[0:n, 512 * half:512 * half + 512], bank[half][0:n, :], h[0:n, 512 * half:512 * half + 512], ALU.add)
                    last.then_inc(s_h2, 1)
                if tick == T_NORM2 + 3:
                    dve.wait_ge(s_rstd2, w + 1)
                    stt(xn[0:n, :], h[0:n, :], stat[0:n, 5:6], ffn_bc[0:n, :], ALU.mult, ALU.mult).then_inc(s_xn2, 1)
                for hh in range(PEER_HEADS):
                    step = tick - T_TOPK - TOPK_TICKS * hh
                    if 0 <= step < 5:
                        topk(w, n, hh, step)
                if tick == T_TOPK + TOPK_TICKS * PEER_HEADS:
                    link(dve.tensor_copy(gsum[0:n, 0, :].unsqueeze(2), gate_n[0:n, :, 0:1]))
                    tt(gate_n[0:n, :, :], gate_n[0:n, :, :], spread(gsum[0:n, 0, :].unsqueeze(2), 2, TOPK), ALU.subtract).then_inc(s_shift, 1)
                if tick == T_TOPK + TOPK_TICKS * PEER_HEADS + 2:
                    dve.wait_ge(s_gate_e, w + 1)
                    link(dve.tensor_reduce(gsum[0:n, 0, :], gate_n[0:n, :, :], AX.X, ALU.add))
                    link(dve.reciprocal(gsum[0:n, 1, :], gsum[0:n, 0, :]))
                    tt(gate_n[0:n, :, :], gate_n[0:n, :, :], spread(gsum[0:n, 1, :].unsqueeze(2), 2, TOPK), ALU.mult).then_inc(s_sel, 1)

            def take_over(w, sample):
                dve.wait_ge(s_sel, w + 1)
                g = gate_n[:, :, :].rearrange("p h k -> p (h k)")
                if sample:
                    for q in range(COPIES):
                        last = dve.tensor_copy(gate[SAMPLE * q:SAMPLE * q + SAMPLE, 0:SAMPLE],
                                               g[0:SAMPLE, :].rearrange("p (c q) -> p c q", q=COPIES)[:, :, q])
                else:
                    dve.wait_ge(s_coef, groups_before(w, sample))
                    last = dve.tensor_copy(gate[:, :], g)
                last.then_inc(s_gate_cur, 1)

            def expert(w, sample, tick):
                before, groups = experts_before(w, sample), groups_before(w, sample)
                if tick < n_experts(sample):
                    place = u_place(tick)
                    if tick == 0:
                        dve.wait_ge(s_xcur, w + 1)
                    dve.wait_ge(s_row[place % RING], (gathers_before(w, sample) + place // RING + 1) * 16)
                    row = ring[:, place % RING, :]
                    stt(row, row, 1.0, xcur[:, :], ALU.mult, ALU.mult, accum_out=dots[:, tick:tick + 1]).then_inc(s_dot, 1)
                if tick % TOPK == TOPK - 1 and tick < n_experts(sample):
                    g = tick // TOPK
                    d = dots[:, TOPK * g:TOPK * g + TOPK]
                    dve.wait_ge(s_dot, before + tick + 1)
                    link(tt(gl_a[:, :], d, d, ALU.mult))
                    link(ts(gl_a[:, :], gl_a[:, :], GELU_CUBIC, 1.0, ALU.mult, ALU.add))
                    link(tt(gl_a[:, :], gl_a[:, :], d, ALU.mult))
                    ts(gl_a[:, :], gl_a[:, :], -50.0, None, ALU.max).then_inc(s_arg, 1)
                    if g == 0:
                        dve.wait_ge(s_gate_cur, w + 1)
                    link(tt(gl_b[:, :], d, gate[:, TOPK * g:TOPK * g + TOPK], ALU.mult))
                if tick and tick % TOPK == 0 and tick <= n_experts(sample):
                    g = tick // TOPK - 1
                    dve.wait_ge(s_gexp, groups + g + 1)
                    link(ts(gl_a[:, :], gl_a[:, :], 1.0, None, ALU.add))
                    link(dve.reciprocal(gl_a[:, :], gl_a[:, :]))
                    tt(coef[:, TOPK * g:TOPK * g + TOPK], gl_a[:, :], gl_b[:, :], ALU.mult).then_inc(s_coef, 1)

            def finish(w, sample):
                n = SAMPLE if sample else P
                dve.wait_ge(s_rstd_y, w + 1)
                rowsT = xT[0:n, :, :].rearrange("p c t -> p (c t)")
                stt(rowsT, rowsT, stat[0:n, 8:9], final_bc[0:n, :], ALU.mult, ALU.mult).then_inc(s_y, 1)

            dve.wait_ge(s_const, 7)
            setup()
            for tick in range(TICKS):
                mixer(0, 0, SAMPLE, True, tick)
            take_over(0, True)
            dve.wait_ge(s_state_out, 64)
            dve.memset(xl[:, :, 0:CONV_W - 1], 0.0)
            dve.memset(hst[:, :], 0.0)
            dve.memset(C[:, :, :], 0.0)
            dve.memset(mst[:, :], 0.0).then_inc(s_reset, 1)
            dve.wait_ge(s_reset, 1)
            for tick in range(TICKS):
                mixer(1, 1, META, False, tick)
            for tick in range(SAMPLE + TOPK):
                expert(0, True, tick)
                for t in range(3 * tick, 3 * tick + 3):
                    mixer(2, 1, P, True, t)
            finish(0, True)
            with dve.Fori(0, BLOCKS - 1) as i:
                restart()
                take_over(i + 1, False)
                for tick in range(TICKS):
                    expert(i + 1, False, tick)
                    mixer(i + 3, i + 2, P, True, tick)
                finish(i + 1, False)
            restart()
            take_over(BLOCKS, False)
            for tick in range(TICKS):
                expert(BLOCKS, False, tick)
            finish(BLOCKS, False)


def kernel(**inputs):
    import concourse.bacc as bacc
    from concourse.bass_utils import run_bass_kernel_spmd

    a = {k: np.asarray(v) for k, v in inputs.items()}

    def channels(x):
        x = x.reshape(x.shape[0], -1, P)
        return np.ascontiguousarray(x.transpose(2, 1, 0))

    def halves(x):
        return np.ascontiguousarray(x.reshape(FT, 2, 64, 64).transpose(1, 2, 0, 3))

    vectors = [a[k][0] for k in ("lru_ba", "lru_bx", "lru_lambda", "mlstm_norm", "conv_b", "norm_mix")]
    ins = {
        "x_prompt": a["x_prompt"][0],
        "x_sample": a["x_sample"][0],
        "meta": a["meta_tokens"],
        "w_in": a["w_in"][0],
        "vecs": np.concatenate([v.reshape(-1, P).T for v in vectors], axis=1),
        "conv_w": channels(a["conv_w"][0]),
        "b_gates": a["b_gates"][0].reshape(2, HEADS).T,
        "lru_wa": halves(a["lru_wa"][0]),
        "lru_wx": halves(a["lru_wx"][0]),
        "w_out": a["w_out"][0],
        "ffn_row": a["norm_ffn"],
        "final_row": a["norm_final"][None],
        "wq": a["peer_wq"][0].reshape(CM, P, 2 * PEER_HEADS, P).transpose(2, 1, 0, 3),
        "keys": np.stack([a["peer_keys1"][0].T, a["peer_keys2"][0].T], axis=1),
        "peer_u": a["peer_u"][0],
        "peer_v": a["peer_v"][0],
        "conv0": channels(a["state_conv"][0, 0]),
        "lru0": a["state_lru"][0, 0].reshape(FT, P).T,
        "c0": np.concatenate([a["state_mlstm_c"][0, 0].transpose(1, 0, 2), a["state_mlstm_n"][0, 0].T[:, :, None]], axis=2),
        "m0": a["state_mlstm_m"][0, 0][:, None],
    }
    ins = {k: np.ascontiguousarray(v) for k, v in ins.items()}
    outs = {
        "y_prompt": (SEQ, D_MODEL),
        "y_sample": (SAMPLE, D_MODEL),
        "conv_out": (2, P, FT, CONV_W - 1),
        "lru_out": (2, P, FT),
        "c_out": (2, P, HEADS, HEAD + 1),
        "m_out": (2, HEADS, 1),
    }
    nc = bacc.Bacc("TRN2", target_bir_lowering=False, num_devices=1, dynamic_dma_scratch_size=4096)
    fp32 = mybir.dt.float32
    aps = [nc.dram_tensor(k, v.shape, fp32, kind="ExternalInput").ap() for k, v in ins.items()]
    aps += [nc.dram_tensor(k, s, fp32, kind="ExternalOutput").ap() for k, s in outs.items()]
    program(nc, *aps)
    r = run_bass_kernel_spmd(nc, [ins], core_ids=[0]).results[0]

    def states(s):
        return (r["conv_out"][s].transpose(2, 1, 0).reshape(1, 1, CONV_W - 1, D_LRU),
                r["lru_out"][s].T.reshape(1, 1, D_LRU),
                r["c_out"][s][:, :, 0:HEAD].transpose(1, 0, 2)[None, None],
                r["c_out"][s][:, :, HEAD].T[None, None],
                r["m_out"][s].reshape(1, 1, HEADS))

    out = (r["y_prompt"][None], r["y_sample"][None], *states(1), *states(0))
    return tuple(np.ascontiguousarray(x) for x in out)
```

```python
import numpy as np
import concourse.bass as bass
from concourse import mybir
from contextlib import ExitStack

D_MODEL = 1024
SEQ = 1024
SAMPLE = 32
META = 16
D_LRU = 512
HEADS = 4
HEAD = 128
CONV_W = 4
D_IN = 2 * D_LRU + 4 * HEADS * HEAD + 2 * HEADS
PEER_HEADS = 8
TOPK = 16
P = 128
CM = D_MODEL // P
FT = D_LRU // P
BLOCKS = SEQ // P
EPS = 1e-6
GELU_CUBIC = 0.044715
GELU_SCALE = -2.0 * (2.0 / np.pi) ** 0.5
COPIES = P // SAMPLE
RING = 8
DIAGS = 4
QUERY_SLOTS = 5
VECS = 5 * FT + CM
MASKED = -1.0e30

HEAD_TICKS = TOPK
BLOCK_TICKS = PEER_HEADS * HEAD_TICKS
QUERY_TICKS = 5
T_QUERY = 1
T_NORM, T_XT, T_XT_OUT = 30, 35, 36
PARTS = (0, 2, 4, 5)
WIDE_PARTS = (0, 2, 3, 5)
OUT_PARTS = WIDE_PARTS + tuple(7 + t for t in WIDE_PARTS)
T_XL, T_GATES, T_GL, T_Q, T_K, T_V, T_O = 37, 43, 45, 52, 59, 66, 73
T_CONV = 44
T_ROWS = 46
T_GELU = 51
T_LRU = 55
T_CHUNK = 74
T_OUT = 91
T_NORM2 = 105
T_QUERY0 = 110
T_MIXER = T_NORM
T_SAMPLE_Q = 30
MIXER_PACE = 5
MIXER_LEAD = 3


def spread(ap, axis, n):
    shape = list(ap.shape)
    shape[axis] = n
    return ap.to_broadcast(shape)


def is_count(v, number):
    return isinstance(v, int) and v == number


def program(nc, x_prompt, x_sample, meta, w_in, vecs, conv_w, b_gates, lru_wa, lru_wx, w_out, ffn_row, final_row,
            wq, keys, peer_u, peer_v, conv0, lru0, c0, m0, y_prompt, y_sample, conv_out, lru_out, c_out, m_out):
    fp32, u32 = mybir.dt.float32, mybir.dt.uint32
    ALU, ACT, AX = mybir.AluOpType, mybir.ActivationFunctionType, mybir.AxisListType
    ctx = ExitStack()
    with ctx:
        def sb(name, shape, dt=fp32):
            return ctx.enter_context(nc.sbuf_tensor(name, shape, dt))

        def sem(name):
            return ctx.enter_context(nc.semaphore(name))

        win = sb("win", [P, CM, D_IN])
        wout = sb("wout", [P, CM, D_MODEL])
        wa = sb("wa", [P, FT, P])
        wx = sb("wx", [P, FT, P])
        keysT = sb("keysT", [P, 2, P])
        ffn_bc = sb("ffn_bc", [P, D_MODEL])
        final_bc = sb("final_bc", [P, D_MODEL])
        vec = sb("vec", [P, VECS])
        cw = sb("cw", [P, FT, CONV_W])
        bg = sb("bg", [HEADS, 2])
        ident = sb("ident", [P, P])
        mask = sb("mask", [P, P])
        rep = sb("rep", [P, SAMPLE])
        iota = sb("iota", [P, TOPK])
        ones4 = sb("ones4", [HEADS, P])
        eps = sb("eps", [P, 1])
        neg = sb("neg", [P, 2 * FT])
        nbf = sb("nbf", [HEADS, 1])
        decay_c = sb("decay_c", [P, 2 * FT])
        sp_t = sb("sp_t", [P, 6, FT])
        ring = sb("ring", [P, RING, D_MODEL])
        xcur = sb("xcur", [P, D_MODEL])
        idx = sb("idx", [P, PEER_HEADS * TOPK], u32)
        gate = sb("gate", [P, PEER_HEADS * TOPK])
        dots = sb("dots", [P, PEER_HEADS * TOPK])
        coef = sb("coef", [P, PEER_HEADS * TOPK])
        gl_a = sb("gl_a", [P, TOPK])
        gl_b = sb("gl_b", [P, TOPK])
        diag = sb("diag", [P, DIAGS, P])
        h = sb("h", [P, D_MODEL])
        xn = sb("xn", [P, D_MODEL])
        xT = sb("xT", [P, CM, P])
        xl = sb("xl", [P, FT, CONV_W - 1 + P])
        G = sb("G", [P, FT, P])
        xc = sb("xc", [P, FT, P])
        qk = sb("qk", [P, 2 * FT, P])
        t34 = sb("t34", [P, 2 * FT, P])
        vt = sb("vt", [P, HEADS, HEAD + 1])
        kw = sb("kw", [P, HEADS, HEAD])
        C = sb("C", [P, HEADS, HEAD + 1])
        hst = sb("hst", [P, FT])
        mst = sb("mst", [HEADS, 1])
        rows_hi = sb("rows_hi", [HEADS, 2, P])
        dg4 = sb("dg4", [HEADS, HEADS])
        cols = sb("cols", [P, 5, HEADS])
        den = sb("den", [P, HEADS])
        stat = sb("stat", [P, 9])
        hstat = sb("hstat", [P, HEADS])
        tops = sb("tops", [P, 2, TOPK])
        topi = sb("topi", [P, 2, TOPK], u32)
        ci = sb("ci", [P, 3, TOPK], u32)
        eh = sb("eh", [P, 2, TOPK])
        gmax = sb("gmax", [P, PEER_HEADS])
        gsum = sb("gsum", [P, PEER_HEADS])
        ginv = sb("ginv", [P, 1])
        qT, kT = qk[:, 0:FT, :], qk[:, FT:2 * FT, :]
        sigo = qk[:, 0:FT, :]
        t3, t4 = t34[:, 0:FT, :], t34[:, FT:2 * FT, :]
        t1 = xn[:, 0:512].rearrange("p (f t) -> p f t", f=FT)
        t2 = xn[:, 512:1024].rearrange("p (f t) -> p f t", f=FT)
        ba, bx, lam, mnorm, convb = (slice(FT * a, FT * a + FT) for a in range(5))
        nmix = slice(5 * FT, 5 * FT + CM)
        wq_buf = [qk, t34]
        q2 = G
        kflat = kw[:, :, :].rearrange("p h d -> p (h d)")
        rows = [kflat[0:HEADS, P * r:P * r + P] for r in range(4)] + [rows_hi[:, 0, :], rows_hi[:, 1, :]]
        choice = [kflat[:, 0:256], kflat[:, 256:512]]
        temps_s, rows_s = ring[:, QUERY_SLOTS + 1, :], ring[:, QUERY_SLOTS + 2, :]
        xT_s = temps_s[:, 0:CM * SAMPLE].rearrange("p (c t) -> p c t", c=CM)
        qrow_s = temps_s[:, 256:512]
        q2_s = temps_s[:, 512:768].rearrange("p (f t) -> p f t", f=2)
        choice_s = [ring[:, QUERY_SLOTS, 0:256], ring[:, QUERY_SLOTS, 256:512]]
        rowbuf = {"xl": rows_s[:, 0:512], "k": rows_s[:, 512:1024], "gates": temps_s[:, 768:768 + 2 * HEADS],
                  "gl": ring[:, QUERY_SLOTS, 0:512], "q": ring[:, QUERY_SLOTS, 512:1024]}
        BOTH = SAMPLE + META

        def wq_s(ft):
            return ring[:, ft % QUERY_SLOTS, :].rearrange("p (c t) -> p c t", c=CM)
        acc = ctx.enter_context(nc.psum_tensor("acc", [P, D_MODEL], fp32))
        bank = [ctx.enter_context(nc.psum_tensor(f"bank{b}", [P, 512], fp32)) for b in range(6)]
        bA, bB, bC, bD, bE, bF = bank

        def by4(b):
            return b[:, :].rearrange("p (f t) -> p f t", f=FT)

        def pair(b):
            return b[:, 0:2 * (HEAD + 1)].rearrange("p (h e) -> p h e", h=2)

        s_small = sem("s_small")
        s_rows_bc = sem("s_rows_bc")
        s_state_in = sem("s_state_in")
        s_win = [sem(f"s_win{g}") for g in range(7)]
        s_wout = sem("s_wout")
        s_x = sem("s_x")
        s_wq = [sem("s_wq0"), sem("s_wq1")]
        s_wq_s = [sem(f"s_wq_s{r}") for r in range(QUERY_SLOTS)]
        s_row = [sem(f"s_row{r}") for r in range(RING)]
        s_y_out = sem("s_y_out")
        s_state_out = sem("s_state_out")
        s_zero = sem("s_zero")
        s_blocks = sem("s_blocks")
        s_const = sem("s_const")
        s_pool = sem("s_pool")
        s_setup = sem("s_setup")
        s_setup_e, s_setup_l, s_setup_a = sem("s_setup_e"), sem("s_setup_l"), sem("s_setup_a")
        s_reset = sem("s_reset")
        s_xcur = sem("s_xcur")
        s_dot, s_arg, s_gexp, s_coef = sem("s_dot"), sem("s_arg"), sem("s_gexp"), sem("s_coef")
        s_diag, s_vsum, s_acc0 = sem("s_diag"), sem("s_vsum"), sem("s_acc0")
        s_acc_out, s_rstd_y, s_y = sem("s_acc_out"), sem("s_rstd_y"), sem("s_y")
        s_xn, s_xt_ps, s_xt = sem("s_xn"), sem("s_xt_ps"), sem("s_xt")
        s_xl_ps, s_xl, s_xc = sem("s_xl_ps"), sem("s_xl"), sem("s_xc")
        s_gl_ps, s_gl, s_gl_arg, s_gl_exp = sem("s_gl_ps"), sem("s_gl"), sem("s_gl_arg"), sem("s_gl_exp")
        s_ri_ps, s_ri_exp, s_r, s_a, s_m2, s_mult, s_lru = (sem(f"s_{n}") for n in ("ri_ps", "ri_exp", "r", "a", "m2", "mult", "lru"))
        s_q_ps, s_q, s_k_ps, s_k, s_v_ps, s_v = (sem(f"s_{n}") for n in ("q_ps", "q", "k_ps", "k", "v_ps", "v"))
        s_g_ps, s_fneg, s_fabs, s_fln, s_mrow, s_rows = (sem(f"s_{n}") for n in ("g_ps", "fneg", "fabs", "fln", "mrow", "rows"))
        s_dg, s_cols_ps, s_cols, s_bc_ps, s_qd, s_wmask, s_w = (sem(f"s_{n}") for n in ("dg", "cols_ps", "cols", "bc_ps", "qd", "wmask", "w"))
        s_kt_ps, s_kw, s_s_ps, s_p, s_num_ps, s_num, s_c_ps, s_c = (sem(f"s_{n}") for n in ("kt_ps", "kw", "s_ps", "p", "num_ps", "num", "c_ps", "c"))
        s_o_ps, s_o, s_hsq, s_hrs, s_ym, s_ym_ps, s_ymT = (sem(f"s_{n}") for n in ("o_ps", "o", "hsq", "hrs", "ym", "ym_ps", "ymT"))
        s_out_ps, s_h2, s_rstd2, s_xn2, s_x2_ps, s_x2 = (sem(f"s_{n}") for n in ("out_ps", "h2", "rstd2", "xn2", "x2_ps", "x2"))
        s_qp_ps, s_q2, s_score, s_topk, s_gmax, s_gate, s_sel = (sem(f"s_{n}") for n in ("qp_ps", "q2", "score", "topk", "gmax", "gate", "sel"))
        s_qs_tile, s_qrow, s_qs_ps, s_q2s, s_score_s = (sem(f"s_{n}") for n in ("qs_tile", "qrow", "qs_ps", "q2s", "score_s"))
        s_rows_ps, s_rowbuf = sem("s_rows_ps"), sem("s_rowbuf")
        s_pool_turn, s_dve_turn, s_sp_turn = sem("s_pool_turn"), sem("s_dve_turn"), sem("s_sp_turn")
        s_dve, s_act = sem("s_dve"), sem("s_act")

        def streams_before(b):
            return 0 if b is None else b + 1

        def experts_before(b):
            return 0 if b is None else b * P + SAMPLE

        def heads_before(b):
            return 0 if b is None else b * PEER_HEADS + SAMPLE // TOPK

        def n_experts(b):
            return SAMPLE if b is None else P

        def column(b, e):
            return P - SAMPLE + e if b is None else e

        def row_of(which, b, e):
            turn, lead = 2 * P // RING, (2 * SAMPLE + TOPK) // RING
            if b is None:
                before, place = 0, 2 * e + TOPK + 1 if which else e if e < TOPK else 2 * e - TOPK
            elif which:
                before, place = lead + b * turn, 2 * e + 1
                if is_count(b, BLOCKS - 1) and e >= P - TOPK:
                    place = e + P - TOPK
            elif e >= TOPK:
                before, place = lead + b * turn, 2 * e - 2 * TOPK
            else:
                before, place = lead + (b - 1) * turn, 2 * (P - TOPK) + 2 * e
            return place % RING, (before + place // RING + 1) * 16

        def rows_count(name):
            return ("xl", "gates", "gl", "q", "k").index(name) + 1

        def projected(v):
            return 1 if is_count(v, 0) or is_count(v, 1) else v

        def tokens_of(v, n):
            return slice(SAMPLE, SAMPLE + n) if is_count(v, 1) else slice(0, n)

        def looped(v):
            return not isinstance(v, int)

        block = ctx.enter_context(nc.Block())

        @block.sync
        def _(sp):
            w_cols = w_in.rearrange("(c p) n -> p c n", p=P)

            def load_win(g):
                lo, hi = 512 * g, min(512 * g + 512, D_IN)
                sp.dma_start(win[:, :, lo:hi], w_cols[:, :, lo:hi]).then_inc(s_win[g], 16)

            def held():
                sp.sem_inc(s_sp_turn, 1)

            def load_wq(b, tiles):
                for ft in tiles:
                    if ft < 2:
                        sp.wait_ge(s_ym_ps, streams_before(b) + 1)
                    else:
                        sp.wait_ge(s_qp_ps, b * 16 + ft - 1)
                    held()
                    sp.dma_start(wq_buf[ft % 2][:, :, :], wq[ft]).then_inc(s_wq[ft % 2], 16)

            def store_states(stream, v, w):
                sp.wait_ge(s_lru, v + 1)
                sp.dma_start(conv_out[stream], xl[:, :, 0:CONV_W - 1]).then_inc(s_state_out, 16)
                sp.dma_start(lru_out[stream], hst[:, :]).then_inc(s_state_out, 16)
                sp.wait_ge(s_c, v + 1)
                sp.dma_start(c_out[stream], C[:, :, :]).then_inc(s_state_out, 16)
                sp.dma_start(m_out[stream], mst[:, :]).then_inc(s_state_out, 16)

            def store_y(b, dst):
                sp.wait_ge(s_y, streams_before(b) + 1)
                held()
                sp.dma_start(dst, xn[0:n_experts(b), :]).then_inc(s_y_out, 16)

            def load_x(b, block):
                sp.wait_ge(s_xcur, streams_before(b))
                held()
                sp.wait_ge(s_y_out, 16 * b)
                held()
                sp.dma_start(xn[:, :], block).then_inc(s_x, 16)

            sp.dma_start(xn[0:SAMPLE, :], x_sample).then_inc(s_x, 16)
            sp.dma_start(xn[SAMPLE:BOTH, :], meta).then_inc(s_x, 16)
            sp.dma_start(vec[:, :], vecs).then_inc(s_small, 16)
            sp.dma_start(cw[:, :, :], conv_w).then_inc(s_small, 16)
            sp.dma_start(bg[:, :], b_gates).then_inc(s_small, 16)
            sp.dma_start(keysT[:, :, :], keys).then_inc(s_small, 16)
            load_win(0)
            sp.dma_start(xl[:, :, 0:CONV_W - 1], conv0).then_inc(s_state_in, 16)
            sp.dma_start(hst[:, :], lru0).then_inc(s_state_in, 16)
            sp.dma_start(C[:, :, :], c0).then_inc(s_state_in, 16)
            sp.dma_start(mst[:, :], m0).then_inc(s_state_in, 16)
            sp.wait_ge(s_zero, 2)
            for half in range(2):
                lo = half * 64
                sp.dma_start(wa[lo:lo + 64, :, lo:lo + 64], lru_wa[half]).then_inc(s_blocks, 16)
                sp.dma_start(wx[lo:lo + 64, :, lo:lo + 64], lru_wx[half]).then_inc(s_blocks, 16)
            for g in (6, 1, 2, 3, 4, 5):
                load_win(g)
            sp.dma_start(ffn_bc[:, :], spread(ffn_row, 0, P)).then_inc(s_rows_bc, 16)
            sp.dma_start(final_bc[:, :], spread(final_row, 0, P)).then_inc(s_rows_bc, 16)
            sp.dma_start(wout[:, :, :], w_out.rearrange("(c p) n -> p c n", p=P)).then_inc(s_wout, 16)
            for ft in range(QUERY_SLOTS):
                sp.dma_start(wq_s(ft), wq[ft]).then_inc(s_wq_s[ft], 16)
            store_states(0, 0, 0)
            for ft in range(QUERY_SLOTS, 2 * PEER_HEADS):
                sp.wait_ge(s_qs_tile, ft - QUERY_SLOTS + 1)
                sp.dma_start(wq_s(ft), wq[ft]).then_inc(s_wq_s[ft % QUERY_SLOTS], 16)
            sp.wait_ge(s_lru, 2)
            sp.dma_start(xn[:, :], x_prompt[0:P, :]).then_inc(s_x, 16)
            load_wq(0, range(10))
            store_y(None, y_sample)
            with sp.Fori(0, BLOCKS - 1) as b:
                load_wq(b, range(10, 12))
                load_x(b + 1, x_prompt[bass.ds(b * P + P, P), :])
                load_wq(b, range(12, 16))
                load_wq(b + 1, range(10))
                store_y(b, y_prompt[bass.ds(b * P, P), :])
            load_wq(BLOCKS - 1, range(10, 16))
            store_states(1, BLOCKS + 1, BLOCKS)
            store_y(BLOCKS - 1, y_prompt[(BLOCKS - 1) * P:BLOCKS * P, :])
            sp.wait_ge(s_state_out, 128)
            sp.wait_ge(s_y_out, 16 * (BLOCKS + 1))

        @block.gpsimd
        def _(pool):
            pool.memset(wa[:, :, :], 0.0).then_inc(s_zero, 1)
            pool.memset(wx[:, :, :], 0.0).then_inc(s_zero, 1)
            pool.memset(ident[:, :], 0.0).then_inc(s_pool, 1)
            pool.memset(mask[:, :], 0.0).then_inc(s_pool, 1)
            pool.memset(rep[:, :], 0.0).then_inc(s_pool, 1)
            pool.memset(ones4[:, :], 1.0).then_inc(s_const, 1)
            pool.memset(eps[:, :], EPS).then_inc(s_const, 1)
            pool.memset(vt[:, :, HEAD:HEAD + 1], 1.0).then_inc(s_const, 1)
            pool.iota(iota[:, :], pattern=[[1, TOPK]], base=0, channel_multiplier=0,
                      allow_small_or_imprecise_dtypes=True).then_inc(s_const, 1)
            pool.wait_ge(s_pool, 3)
            pool.affine_select(out=ident[:, :], in_=ident[:, :], compare_op=ALU.not_equal, fill=1.0, base=0,
                               pattern=[[-1, P]], channel_multiplier=1).then_inc(s_const, 1)
            pool.affine_select(out=mask[:, :], in_=mask[:, :], compare_op=ALU.is_ge, fill=MASKED, base=0,
                               pattern=[[1, P]], channel_multiplier=-1).then_inc(s_const, 1)
            for q in range(COPIES):
                pool.affine_select(out=rep[:, :], in_=rep[:, :], compare_op=ALU.not_equal, fill=1.0,
                                   base=-SAMPLE * q, pattern=[[-1, SAMPLE]], channel_multiplier=1).then_inc(s_pool, 1)
                pool.wait_ge(s_pool, 4 + q)
            pool.memset(diag[:, :, :], 0.0).then_inc(s_const, 1)

            U, V = 0, 1

            def gathers(order, held):
                for place, (which, b, e) in enumerate(order):
                    if which == U and e % TOPK == 0:
                        pool.wait_ge(s_sel, heads_before(b) + e // TOPK + 1)
                    old = order[place - RING] if place >= RING else held[place] if held else None
                    if old:
                        pool.wait_ge((s_dot, s_vsum)[old[0]], experts_before(old[1]) + old[2] + 1)
                    if b is None and which == U and e == QUERY_SLOTS:
                        pool.wait_ge(s_sel, SAMPLE // TOPK)
                        pool.wait_ge(s_k_ps, 2)
                    pool.sem_inc(s_pool_turn, 1)
                    slot, _ = row_of(which, b, e)
                    pool.indirect_dma_start(
                        out=ring[:, slot, :], out_offset=None, in_=(peer_u, peer_v)[which],
                        in_offset=bass.IndirectOffsetOnAxis(ap=idx[:, column(b, e):column(b, e) + 1], axis=0)).then_inc(s_row[slot], 16)

            def side_by_side(b, ticks):
                return [x for t in ticks for x in ((U, b, t), (V, b, t - TOPK))]

            def over(b):
                last = (None, SAMPLE - TOPK) if is_count(b, 0) else (b - 1, P - TOPK)
                return [x for t in range(TOPK) for x in ((U, b, t), (V, last[0], last[1] + t))]

            pool.wait_ge(s_qs_tile, 2 * PEER_HEADS)
            first = [(U, None, t) for t in range(TOPK)] + side_by_side(None, range(TOPK, SAMPLE))
            gathers(first + over(0), None)
            with pool.Fori(0, BLOCKS - 1) as b:
                gathers(side_by_side(b, range(TOPK, P)) + over(b + 1), over(b)[-RING:])
            b = BLOCKS - 1
            gathers(side_by_side(b, range(TOPK, P)) + [(V, b, j) for j in range(P - TOPK, P)], over(b)[-RING:])

        @block.tensor
        def _(pe):
            def mm(out, lhsT, rhs, start=True, stop=True):
                return nc.tensor.matmul(out, lhsT, rhs, start=start, stop=stop)

            def project(out, lo, width, n):
                for c in range(CM):
                    last = mm(out, win[:, c, lo:lo + width], xT[:, c, 0:n], start=c == 0, stop=c == CM - 1)
                return last

            def project_rows(out, lo, width, n):
                for c in range(CM):
                    last = mm(out, xT[:, c, 0:n], win[:, c, lo:lo + width], start=c == 0, stop=c == CM - 1)
                last.then_inc(s_rows_ps, 1)

            def project_part(v, n, b, lo, part, name):
                if n == P:
                    return project(by4(b)[:, part, 0:n], lo + P * part, P, n)
                if part == 0 and v == 0:
                    project_rows(b[0:BOTH, :], lo, 512, BOTH)
                if part == FT - 1:
                    pe.wait_ge(s_rowbuf, rows_count(name))
                    mine = tokens_of(v, n)
                    for f in range(FT):
                        last = nc.tensor.transpose(by4(b)[:, f, 0:n], rowbuf[name][mine, P * f:P * f + P], ident[mine, mine])
                    return last

            def mixer(v, w, n, full, tick):
                if tick == T_XT:
                    if not is_count(v, 0):
                        pe.wait_ge(s_c, v)
                        pe.wait_ge(s_lru, v)
                    else:
                        pe.wait_ge(s_const, 7)
                    if looped(v):
                        pe.wait_ge(s_q2, (w - 1) * 16)
                    if full:
                        pe.wait_ge(s_xn, projected(v))
                        m = BOTH if is_count(v, 0) else n
                        for c in range(CM):
                            last = nc.tensor.transpose(by4(bank[4 + c // 4])[:, c % 4, 0:m], xn[0:m, c * P:(c + 1) * P], ident[0:m, 0:m])
                        last.then_inc(s_xt_ps, 1)
                if tick - T_XL in PARTS:
                    f = PARTS.index(tick - T_XL)
                    if f == 0:
                        pe.wait_ge(s_win[0], 16)
                        pe.wait_ge(s_xt, projected(v))
                        if looped(v):
                            pe.wait_ge(s_topk, 2 + (w - 1) * PEER_HEADS)
                    last = project_part(v, n, bC, 0, f, "xl")
                    if f == FT - 1:
                        last.then_inc(s_xl_ps, 1)
                if tick == T_GATES:
                    pe.wait_ge(s_win[6], 16)
                    if n == P:
                        project(bB[0:HEADS, 0:n], D_IN - 2 * HEADS, HEADS, n)
                    elif full:
                        project_rows(bB[0:BOTH, 0:2 * HEADS], D_IN - 2 * HEADS, 2 * HEADS, BOTH)
                if tick == T_GATES + 1:
                    if n == P:
                        last = project(bB[0:HEADS, P:P + n], D_IN - HEADS, HEADS, n)
                    else:
                        pe.wait_ge(s_rowbuf, rows_count("gates"))
                        mine = tokens_of(v, n)
                        for half in range(2):
                            last = nc.tensor.transpose(bB[0:HEADS, P * half:P * half + n], rowbuf["gates"][mine, HEADS * half:HEADS * half + HEADS],
                                                       ident[mine, mine])
                    last.then_inc(s_g_ps, 1)
                if full and tick - T_GL in PARTS:
                    f = PARTS.index(tick - T_GL)
                    if f == 0:
                        pe.wait_ge(s_win[1], 16)
                    last = project_part(v, n, bD, 512, f, "gl")
                    if f == FT - 1:
                        last.then_inc(s_gl_ps, 1)
                if full and tick - T_Q in PARTS:
                    f = PARTS.index(tick - T_Q)
                    if f == 0:
                        pe.wait_ge(s_win[2], 16)
                    last = project_part(v, n, bE, 1024, f, "q")
                    if f == FT - 1:
                        last.then_inc(s_q_ps, 1)
                if tick - T_K in PARTS:
                    f = PARTS.index(tick - T_K)
                    if f == 0:
                        pe.wait_ge(s_win[3], 16)
                    last = project_part(v, n, bF, 1536, f, "k")
                    if f == FT - 1:
                        last.then_inc(s_k_ps, 1)
                if tick == T_LRU:
                    if is_count(v, 0):
                        pe.wait_ge(s_blocks, 64)
                    pe.wait_ge(s_xc, v + 1)
                    pe.wait_ge(s_mrow, v + 1)
                    for f in range(FT):
                        mm(by4(bC)[:, f, 0:n], wa[:, f, :], xc[:, f, 0:n])
                    for f in range(FT):
                        last = mm(by4(bB)[:, f, 0:n], wx[:, f, :], xc[:, f, 0:n])
                    last.then_inc(s_ri_ps, 1)
                if full and tick - T_V in WIDE_PARTS:
                    part = WIDE_PARTS.index(tick - T_V)
                    if part == 0:
                        pe.wait_ge(s_win[4], 16)
                    m = BOTH if is_count(v, 0) else n
                    for c in (2 * part, 2 * part + 1):
                        last = mm(bA[0:m, :], xT[:, c, 0:m], win[:, c, 2048:2560], start=c == 0, stop=c == CM - 1)
                    if part == 3:
                        last.then_inc(s_v_ps, 1)
                if tick == T_V + 4:
                    pe.wait_ge(s_k, v + 1)
                    for f in range(HEADS):
                        if is_count(v, 1):
                            last = mm(by4(bF)[tokens_of(v, n), f, :], kT[:, f, 0:n], ident[:, :])
                        else:
                            last = nc.tensor.transpose(by4(bF)[0:n, f, :], kT[:, f, 0:n], ident[:, :])
                    last.then_inc(s_kt_ps, 1)
                if tick == T_V + 1:
                    if full:
                        pe.wait_ge(s_gl, w + 1)
                    pe.wait_ge(s_rows, v + 1)
                    pe.wait_ge(s_dg, v + 1)
                    for a, r in enumerate((3, 1, 2)):
                        mm(bD[tokens_of(v, n), HEADS * a:HEADS * a + HEADS], rows[r][:, 0:n], ident[0:HEADS, 0:HEADS])
                    mm(bD[:, 16:20], ones4[:, :], dg4[:, :]).then_inc(s_cols_ps, 1)
                if full and tick - T_O in WIDE_PARTS:
                    part = WIDE_PARTS.index(tick - T_O)
                    if part == 0:
                        pe.wait_ge(s_win[5], 16)
                        pe.wait_ge(s_q, w + 1)
                    for c in (2 * part, 2 * part + 1):
                        last = mm(bE[0:n, :], xT[:, c, 0:n], win[:, c, 2560:3072], start=c == 0, stop=c == CM - 1)
                    if part == 3:
                        last.then_inc(s_o_ps, 1)
                if full and tick == T_CHUNK:
                    pe.wait_ge(s_v, projected(v))
                    pe.wait_ge(s_ri_exp, v + 1)
                    for f in range(HEADS):
                        sel = spread(ident[0:HEADS, f:f + 1], 1, P)
                        mm(by4(bA)[:, f, 0:n], sel, rows[5][:, 0:n])
                        last = mm(by4(bB)[:, f, 0:n], sel, rows[4][:, 0:n])
                    last.then_inc(s_bc_ps, 1)
                if full and tick == T_CHUNK + 3:
                    pe.wait_ge(s_lru, v + 1)
                    for f in range(HEADS):
                        last = mm(by4(bC)[0:n, f, 0:n], kT[:, f, 0:n], qT[:, f, 0:n])
                    last.then_inc(s_s_ps, 1)
                if full and tick == T_CHUNK + 7:
                    pe.wait_ge(s_qd, w + 1)
                    pe.wait_ge(s_p, w + 1)
                    for f in range(HEADS):
                        out = pair(bank[f // 2])[0:n, f % 2, :]
                        mm(out, t3[0:n, f, 0:n], vt[0:n, f, :], stop=False)
                        last = mm(out, t2[:, f, 0:n], C[:, f, :], start=False)
                    last.then_inc(s_num_ps, 1)
                if tick == T_CHUNK + 8:
                    pe.wait_ge(s_kw, v + 1)
                    pe.wait_ge(s_cols, v + 1)
                    pe.wait_ge(s_v, projected(v))
                    pe.wait_ge(s_lru, v + 1)
                    for f in range(HEADS):
                        last = mm(pair(bank[2 + f // 2])[:, f % 2, :], kw[tokens_of(v, n), f, :], vt[tokens_of(v, n), f, :])
                    last.then_inc(s_c_ps, 1)
                if not full:
                    return
                if tick == T_OUT - 2:
                    pe.wait_ge(s_ym, w + 1)
                    for f in range(HEADS):
                        last = nc.tensor.transpose(by4(bF)[:, f, 0:n], t1[0:n, f, :], ident[0:n, 0:n])
                    last.then_inc(s_ym_ps, 1)
                if tick - T_OUT in OUT_PARTS:
                    c = OUT_PARTS.index(tick - T_OUT)
                    if c == 0:
                        pe.wait_ge(s_wout, 16)
                        pe.wait_ge(s_ymT, w + 1)
                        pe.wait_ge(s_num, w + 1)
                        pe.wait_ge(s_lru, v + 1)
                    y = G[:, c, 0:n] if c < FT else xc[:, c - FT, 0:n]
                    for half in range(2):
                        last = mm(bank[half][0:n, :], y, wout[:, c, 512 * half:512 * half + 512], start=c == 0, stop=c == CM - 1)
                    if c == CM - 1:
                        last.then_inc(s_out_ps, 1)
                if tick == T_NORM2 + 3:
                    pe.wait_ge(s_xn2, w + 1)
                    pe.wait_ge(s_c, v + 1)
                    for c in range(CM):
                        last = nc.tensor.transpose(by4(bank[2 + c // 4])[:, c % 4, 0:n], xn[0:n, c * P:(c + 1) * P], ident[0:n, 0:n])
                    last.then_inc(s_x2_ps, 1)

            def query(b, head, step):
                half, part = divmod(step, 2)
                if not 0 <= step < 4:
                    return
                ft = 2 * head + half
                if part == 0:
                    if ft == 0:
                        pe.wait_ge(s_x2, streams_before(b) + 1)
                    if ft >= 2:
                        pe.wait_ge(s_q2, b * 16 + ft - 1)
                    pe.wait_ge(s_wq[half], b * 128 + 16 * head + 16)
                    for c in range(CM):
                        last = mm(bank[4 + half][:, 0:P], wq_buf[half][:, c, :], xT[:, c, :], start=c == 0, stop=c == CM - 1)
                    last.then_inc(s_qp_ps, 1)
                else:
                    if half == 0 and head >= 2:
                        pe.wait_ge(s_topk, heads_before(b) + head - 1)
                    pe.wait_ge(s_q2, b * 16 + ft + 1)
                    mm(bank[2 * (head % 2) + half][:, 0:P], q2[:, half, :], keysT[:, half, :]).then_inc(s_score, 1)

            def query_sample(tick):
                ft = tick - T_SAMPLE_Q
                if 0 <= ft < 2 * PEER_HEADS:
                    if ft == 0:
                        pe.wait_ge(s_x2, 1)
                    pe.wait_ge(s_wq_s[ft % QUERY_SLOTS], ft // QUERY_SLOTS * 16 + 16)
                    group, at = divmod(ft, 2 * COPIES)
                    q, half = divmod(at, 2)
                    out = acc[SAMPLE * q:SAMPLE * q + SAMPLE, 512 * group + P * half:512 * group + P * half + P]
                    for c in range(CM):
                        last = mm(out, xT_s[:, c, :], wq_s(ft)[:, c, :], start=c == 0, stop=c == CM - 1)
                    last.then_inc(s_qs_tile, 1)
                for group in range(2):
                    if tick == T_SAMPLE_Q + 8 * group + 9:
                        pe.wait_ge(s_qrow, group + 1)
                        for half in range(2):
                            last = nc.tensor.transpose(acc[:, 512 * group + 256 + P * half:512 * group + 256 + P * half + P],
                                                       qrow_s[:, P * half:P * half + P], ident[:, :])
                        last.then_inc(s_qs_ps, 1)
                    if tick == T_SAMPLE_Q + 8 * group + 11:
                        pe.wait_ge(s_q2s, group + 1)
                        for half in range(2):
                            last = mm(acc[:, 512 * group + P * half:512 * group + P * half + P], q2_s[:, half, :], keysT[:, half, :])
                        last.then_inc(s_score_s, 1)

            def take_up(b):
                n = n_experts(b)
                pe.wait_ge(s_h2, streams_before(b) + 1)
                if b is None:
                    pe.wait_ge(s_topk, 2)
                else:
                    pe.wait_ge(s_acc_out, streams_before(b))
                for half in range(2):
                    last = mm(acc[0:n, 512 * half:512 * half + 512], ident[0:n, 0:n], h[0:n, 512 * half:512 * half + 512], stop=False)
                last.then_inc(s_acc0, 1)

            def expert_sum(b, j):
                n = n_experts(b)
                slot, arrived = row_of(1, b, j)
                pe.wait_ge(s_row[slot], arrived)
                pe.wait_ge(s_diag, experts_before(b) + j + 1)
                for half in range(2):
                    last = mm(acc[0:n, 512 * half:512 * half + 512], diag[:, j % DIAGS, 0:n],
                              ring[:, slot, 512 * half:512 * half + 512], start=False, stop=j == n - 1)
                last.then_inc(s_vsum, 1)

            def beside(b, tick, more):
                for head in range(1, PEER_HEADS):
                    query(b, head, tick - T_QUERY - QUERY_TICKS * (head - 1))
                if more:
                    mixer(b + 3, b + 2, P, True, tick)
                    query(b + 1, 0, tick - T_QUERY0)

            for tick in range(T_MIXER, BLOCK_TICKS):
                mixer(0, 0, SAMPLE, True, tick)
            for tick in range(T_MIXER, BLOCK_TICKS):
                mixer(1, 1, META, False, tick)
                query_sample(tick)
            take_up(None)
            for step in range(TOPK + MIXER_LEAD):
                if step >= MIXER_LEAD:
                    expert_sum(None, step - MIXER_LEAD)
                for t in range(T_MIXER + MIXER_PACE * step, T_MIXER + MIXER_PACE * (step + 1)):
                    mixer(2, 1, P, True, t)
                    query(0, 0, t - T_QUERY0)
            for tick in range(TOPK):
                expert_sum(None, SAMPLE - TOPK + tick)
                beside(0, tick, False)
            take_up(0)
            with pe.Fori(0, BLOCKS - 1) as b:
                for tick in range(TOPK, BLOCK_TICKS):
                    expert_sum(b, tick - TOPK)
                    beside(b, tick, True)
                for tick in range(TOPK):
                    expert_sum(b, P - TOPK + tick)
                    beside(b + 1, tick, False)
                take_up(b + 1)
            b = BLOCKS - 1
            for tick in range(TOPK, BLOCK_TICKS):
                expert_sum(b, tick - TOPK)
                beside(b, tick, False)
            for j in range(P - TOPK, P):
                expert_sum(b, j)

        @block.scalar
        def _(act):
            count = [0]

            def link(ins):
                count[0] += 1
                ins.then_inc(s_act, 1)
                act.wait_ge(s_act, count[0])

            def restart():
                act.sem_clear(s_act)
                count[0] = 0

            def a(out, in_, func, **kw):
                return nc.scalar.activation(out, in_, func, **kw)

            def rstd(n, col, width):
                link(a(stat[0:n, col + 1:col + 2], stat[0:n, col:col + 1], ACT.Ln, scale=1.0 / width, bias=eps[0:n, :]))
                return a(stat[0:n, col + 2:col + 3], stat[0:n, col + 1:col + 2], ACT.Exp, scale=-0.5)

            def rows_out(b, width, name):
                act.wait_ge(s_rows_ps, rows_count(name))
                a(rowbuf[name][0:BOTH, :], b[0:BOTH, 0:width], ACT.Copy).then_inc(s_rowbuf, 1)

            def mixer(v, w, n, full, tick):
                m = BOTH if is_count(v, 0) else n
                if is_count(v, 0):
                    if tick == T_XL:
                        rows_out(bC, 512, "xl")
                    if tick == T_GATES:
                        rows_out(bB, 2 * HEADS, "gates")
                    if tick == T_GL:
                        rows_out(bD, 512, "gl")
                    if tick == T_Q:
                        rows_out(bE, 512, "q")
                    if tick == T_K:
                        rows_out(bF, 512, "k")
                if full and tick == T_NORM:
                    act.wait_ge(s_x, 32 if is_count(v, 0) else 16 * v + 16)
                    junk = h[:, :] if n == P else t34[0:m, :, :].rearrange("p f t -> p (f t)")
                    if n == P:
                        act.wait_ge(s_acc0, w)
                    link(a(junk, xn[0:m, :], ACT.Square, accum_out=stat[0:m, 0:1]))
                    a(h[0:n, :], xn[0:n, :], ACT.Copy)
                    link(rstd(m, 0, D_MODEL))
                    a(xn[0:m, :], xn[0:m, :], ACT.Copy, scale=stat[0:m, 2:3]).then_inc(s_xn, 1)
                if full and tick == T_XT_OUT:
                    act.wait_ge(s_small, 64)
                    act.wait_ge(s_xt_ps, projected(v))
                    for c in range(CM):
                        last = a(xT[:, c, 0:m], by4(bank[4 + c // 4])[:, c % 4, 0:m], ACT.Copy, scale=vec[:, nmix][:, c:c + 1])
                    last.then_inc(s_xt, 1)
                if tick == T_XL + 5:
                    if is_count(v, 0):
                        act.wait_ge(s_state_in, 64)
                    if is_count(v, 1):
                        act.wait_ge(s_reset, 1)
                    act.wait_ge(s_xl_ps, v + 1)
                    a(xl[:, :, CONV_W - 1:CONV_W - 1 + n], by4(bC)[:, :, 0:n], ACT.Copy).then_inc(s_xl, 1)
                if tick == T_ROWS - 1:
                    act.wait_ge(s_g_ps, v + 1)
                    if looped(v):
                        act.wait_ge(s_sel, w * PEER_HEADS - 6)
                    act.wait_ge(s_setup, 1)
                    a(rows[0][:, 0:n], bB[0:HEADS, P:P + n], ACT.Identity, scale=-1.0, bias=nbf[:, :]).then_inc(s_fneg, 1)
                if tick == T_ROWS + 1:
                    act.wait_ge(s_fabs, v + 1)
                    link(a(rows[1][:, 0:n], rows[1][:, 0:n], ACT.Exp, scale=-1.0))
                    a(rows[1][:, 0:n], rows[1][:, 0:n], ACT.Ln, bias=1.0).then_inc(s_fln, 1)
                if full and tick == T_GELU:
                    act.wait_ge(s_gl_ps, w + 1)
                    a(G[:, :, 0:n], by4(bD)[:, :, 0:n], ACT.Copy)
                    a(t3[:, :, 0:n], by4(bD)[:, :, 0:n], ACT.Square).then_inc(s_gl, 1)
                if full and tick == T_GELU + 2:
                    act.wait_ge(s_gl_arg, w + 1)
                    a(t3[:, :, 0:n], t3[:, :, 0:n], ACT.Exp, scale=GELU_SCALE).then_inc(s_gl_exp, 1)
                if tick == T_ROWS + 3:
                    act.wait_ge(s_mrow, v + 1)
                    a(rows[1][:, 0:n], rows[0][:, 0:n], ACT.Exp, scale=-1.0)
                    a(rows[2][:, 0:n], rows[3][:, 0:n], ACT.Exp, bias=rows[5][:, n - 1:n])
                    a(rows[4][:, 0:n], rows[4][:, 0:n], ACT.Exp, scale=-1.0, bias=mst[:, :]).then_inc(s_rows, 1)
                if full and tick == T_Q + 6:
                    act.wait_ge(s_q_ps, w + 1)
                    a(qT[:, :, 0:n], by4(bE)[:, :, 0:n], ACT.Copy).then_inc(s_q, 1)
                if tick == T_K + 7:
                    act.wait_ge(s_k_ps, v + 1)
                    a(kT[:, :, 0:n], by4(bF)[:, :, 0:n], ACT.Copy, scale=float(HEAD) ** -0.5).then_inc(s_k, 1)
                if tick == T_LRU + 1:
                    act.wait_ge(s_ri_ps, v + 1)
                    for f in range(FT):
                        a(t1[:, f, 0:n], by4(bC)[:, f, 0:n], ACT.Exp, scale=-1.0, bias=neg[:, f:f + 1])
                    for f in range(FT):
                        last = a(t2[:, f, 0:n], by4(bB)[:, f, 0:n], ACT.Exp, scale=-1.0, bias=neg[:, FT + f:FT + f + 1])
                    last.then_inc(s_ri_exp, 1)
                if tick == T_LRU + 3:
                    act.wait_ge(s_r, v + 1)
                    for f in range(FT):
                        last = a(t3[:, f, 0:n], t1[:, f, 0:n], ACT.Exp, scale=decay_c[:, f:f + 1])
                    last.then_inc(s_a, 1)
                if full and tick == T_V + 6:
                    act.wait_ge(s_v_ps, projected(v))
                    a(vt[0:m, :, 0:HEAD], by4(bA)[0:m, :, :], ACT.Copy).then_inc(s_v, 1)
                if tick == T_LRU + 10:
                    act.wait_ge(s_m2, v + 1)
                    link(a(t1[:, :, 0:n], t1[:, :, 0:n], ACT.Ln))
                    a(t1[:, :, 0:n], t1[:, :, 0:n], ACT.Exp, scale=0.5).then_inc(s_mult, 1)
                if tick == T_V + 5:
                    act.wait_ge(s_cols_ps, v + 1)
                    a(cols[tokens_of(v, n), 0:3, :], bD[tokens_of(v, n), 0:12].rearrange("p (a h) -> p a h", a=3), ACT.Copy)
                    a(cols[:, 4, :], bD[:, 16:20], ACT.Copy).then_inc(s_cols, 1)
                if full and tick == T_CHUNK + 2:
                    act.wait_ge(s_wmask, w + 1)
                    act.wait_ge(s_cols, v + 1)
                    for f in range(HEADS):
                        last = a(t3[0:n, f, 0:n], t3[0:n, f, 0:n], ACT.Exp, bias=cols[0:n, 0, f:f + 1])
                    last.then_inc(s_w, 1)
                if full and tick == T_CHUNK + 8:
                    act.wait_ge(s_o_ps, w + 1)
                    act.wait_ge(s_num_ps, w + 1)
                    a(sigo[0:n, :, :], by4(bE)[0:n, :, :], ACT.Exp, scale=-1.0).then_inc(s_o, 1)
                if full and tick == T_CHUNK + 12:
                    act.wait_ge(s_hsq, w + 1)
                    link(a(hstat[0:n, :], hstat[0:n, :], ACT.Ln, scale=1.0 / HEAD, bias=eps[0:n, :]))
                    a(hstat[0:n, :], hstat[0:n, :], ACT.Exp, scale=-0.5).then_inc(s_hrs, 1)
                if full and tick == T_OUT - 1:
                    act.wait_ge(s_ym_ps, w + 1)
                    for f in range(HEADS):
                        last = a(xc[:, f, 0:n], by4(bF)[:, f, 0:n], ACT.Copy, scale=vec[:, mnorm][:, f:f + 1])
                    last.then_inc(s_ymT, 1)
                if full and tick == T_NORM2 + 1:
                    act.wait_ge(s_h2, w + 1)
                    link(a(xn[0:n, :], h[0:n, :], ACT.Square, accum_out=stat[0:n, 3:4]))
                    rstd(n, 3, D_MODEL).then_inc(s_rstd2, 1)
                if full and tick == T_NORM2 + 4:
                    act.wait_ge(s_x2_ps, w + 1)
                    to = xT_s if is_count(v, 0) else xT
                    a(to[:, 0:4, 0:n], by4(bC)[:, :, 0:n], ACT.Copy)
                    a(to[:, 4:8, 0:n], by4(bD)[:, :, 0:n], ACT.Copy).then_inc(s_x2, 1)

            def weigh(hh, chosen):
                act.wait_ge(s_gmax, chosen)
                g = gate[:, TOPK * hh:TOPK * hh + TOPK]
                a(g, g, ACT.Exp, bias=gmax[:, hh:hh + 1], accum_out=gsum[:, hh:hh + 1]).then_inc(s_gate, 1)

            def query(b, head, step):
                half = (step - 1) // 2
                if step in (1, 3):
                    ft = 2 * head + half
                    act.wait_ge(s_qp_ps, b * 16 + ft + 1)
                    if ft >= 2:
                        act.wait_ge(s_score, b * 16 + ft - 1)
                    a(q2[:, half, :], bank[4 + half][:, 0:P], ACT.Copy).then_inc(s_q2, 1)
                if step == 7:
                    weigh(head, heads_before(b) + head + 1)

            def query_sample(tick):
                for group in range(2):
                    if tick == T_SAMPLE_Q + 8 * group + 8:
                        act.wait_ge(s_qs_tile, 8 * group + 8)
                        a(qrow_s, acc[:, 512 * group:512 * group + 256], ACT.Copy).then_inc(s_qrow, 1)
                    if tick == T_SAMPLE_Q + 8 * group + 10:
                        act.wait_ge(s_qs_ps, group + 1)
                        a(q2_s[:, :, :], acc[:, 512 * group + 256:512 * group + 512].rearrange("p (f t) -> p f t", f=2),
                          ACT.Copy).then_inc(s_q2s, 1)
                    if tick == T_SAMPLE_Q + 8 * group + 15:
                        weigh(PEER_HEADS - 2 + group, group + 1)

            def take_over(b):
                act.wait_ge(s_xn2, streams_before(b) + 1)
                act.wait_ge(s_x2, streams_before(b) + 1)
                if b is None:
                    for q in range(COPIES):
                        last = a(xcur[SAMPLE * q:SAMPLE * q + SAMPLE, :], xn[0:SAMPLE, :], ACT.Copy)
                else:
                    act.wait_ge(s_dot, experts_before(b))
                    last = a(xcur[:, :], xn[:, :], ACT.Copy)
                last.then_inc(s_xcur, 1)

            def gelu_exp(b, g):
                act.wait_ge(s_arg, heads_before(b) + g + 1)
                a(gl_a[:, :], gl_a[:, :], ACT.Exp, scale=GELU_SCALE).then_inc(s_gexp, 1)

            def diagonal(b, j):
                if j % TOPK == 0:
                    act.wait_ge(s_coef, heads_before(b) + j // TOPK + 1)
                if b is not None or j >= DIAGS:
                    act.wait_ge(s_vsum, experts_before(b) + j - DIAGS + 1)
                a(diag[:, j % DIAGS, 0:n_experts(b)], rep[:, :] if b is None else ident[:, :], ACT.Copy,
                  scale=coef[:, column(b, j):column(b, j) + 1]).then_inc(s_diag, 1)

            def finish(b):
                n = n_experts(b)
                act.wait_ge(s_vsum, experts_before(b) + n)
                y = xn[0:n, :]
                link(a(y, acc[0:n, :], ACT.Square, accum_out=stat[0:n, 6:7]))
                a(y, acc[0:n, :], ACT.Copy).then_inc(s_acc_out, 1)
                rstd(n, 6, D_MODEL).then_inc(s_rstd_y, 1)

            def beside(b, tick, more):
                for head in range(1, PEER_HEADS):
                    query(b, head, tick - T_QUERY - QUERY_TICKS * (head - 1))
                if more:
                    mixer(b + 3, b + 2, P, True, tick)
                    query(b + 1, 0, tick - T_QUERY0)

            nc.scalar.preload_act_table_set("natural_log_exp_and_others")
            act.wait_ge(s_const, 7)
            act.wait_ge(s_setup_a, 1)
            a(sp_t[:, 1, :], sp_t[:, 1, :], ACT.Exp, scale=-1.0).then_inc(s_setup_e, 1)
            act.wait_ge(s_setup_e, 1)
            a(sp_t[:, 2, :], sp_t[:, 1, :], ACT.Ln, bias=1.0).then_inc(s_setup_l, 1)
            for tick in range(T_MIXER, BLOCK_TICKS):
                mixer(0, 0, SAMPLE, True, tick)
            take_over(None)
            for tick in range(T_MIXER, BLOCK_TICKS):
                mixer(1, 1, META, False, tick)
                query_sample(tick)
            for step in range(TOPK + MIXER_LEAD):
                if step == MIXER_LEAD:
                    gelu_exp(None, 0)
                if step >= MIXER_LEAD:
                    diagonal(None, step - MIXER_LEAD)
                for t in range(T_MIXER + MIXER_PACE * step, T_MIXER + MIXER_PACE * (step + 1)):
                    mixer(2, 1, P, True, t)
                    query(0, 0, t - T_QUERY0)
            take_over(0)
            gelu_exp(None, 1)
            for tick in range(TOPK):
                diagonal(None, SAMPLE - TOPK + tick)
                beside(0, tick, False)
            finish(None)
            with act.Fori(0, BLOCKS - 1) as b:
                restart()
                for tick in range(TOPK, BLOCK_TICKS):
                    if tick % TOPK == 0:
                        gelu_exp(b, tick // TOPK - 1)
                    diagonal(b, tick - TOPK)
                    beside(b, tick, True)
                take_over(b + 1)
                gelu_exp(b, PEER_HEADS - 1)
                for tick in range(TOPK):
                    diagonal(b, P - TOPK + tick)
                    beside(b + 1, tick, False)
                finish(b)
            restart()
            b = BLOCKS - 1
            for tick in range(TOPK, BLOCK_TICKS + TOPK):
                if tick % TOPK == 0:
                    gelu_exp(b, tick // TOPK - 1)
                diagonal(b, tick - TOPK)
                if tick < BLOCK_TICKS:
                    beside(b, tick, False)
            finish(b)

        @block.vector
        def _(dve):
            count = [0]

            def link(ins):
                count[0] += 1
                ins.then_inc(s_dve, 1)
                dve.wait_ge(s_dve, count[0])
                return ins

            def held():
                dve.sem_inc(s_dve_turn, 1)

            def restart():
                dve.sem_clear(s_dve)
                count[0] = 0

            tt, ts, stt = dve.tensor_tensor, dve.tensor_scalar, dve.scalar_tensor_tensor

            def setup():
                dve.wait_ge(s_small, 64)
                link(ts(sp_t[:, 0, :], vec[:, lam], -1.0, None, ALU.mult))
                stt(sp_t[:, 1, :], sp_t[:, 0, :], -1.0, sp_t[:, 0, :], ALU.mult, ALU.max).then_inc(s_setup_a, 1)
                ts(neg[:, :], vec[:, 0:2 * FT], -1.0, None, ALU.mult)
                ts(nbf[:, :], bg[:, 1:2], -1.0, None, ALU.mult)
                dve.wait_ge(s_setup_l, 1)
                e, ln, z, z2, p = (sp_t[:, k, :] for k in (1, 2, 3, 4, 5))
                link(ts(z, e, 2.0, None, ALU.add))
                link(dve.reciprocal(z, z))
                link(tt(z, z, e, ALU.mult))
                link(tt(z2, z, z, ALU.mult))
                link(ts(p, z2, 1.0 / 7, 1.0 / 5, ALU.mult, ALU.add))
                link(tt(p, p, z2, ALU.mult))
                link(ts(p, p, 1.0 / 3, None, ALU.add))
                link(tt(p, p, z2, ALU.mult))
                link(ts(p, p, 1.0, 2.0, ALU.add, ALU.mult))
                link(tt(p, p, z, ALU.mult))
                link(ts(z2.bitcast(u32), e, 0.2, None, ALU.is_lt))
                link(dve.copy_predicated(ln, z2.bitcast(u32), p))
                link(stt(ln, sp_t[:, 0, :], 0.0, ln, ALU.max, ALU.add))
                ts(decay_c[:, 0:FT], ln, -8.0, None, ALU.mult)
                ts(decay_c[:, FT:2 * FT], ln, 16.0, None, ALU.mult).then_inc(s_setup, 1)

            def top16(values, work, out_v, out_i):
                link(dve.max(out_v[:, 0:8], values))
                link(dve.match_replace(work, out_v[:, 0:8], values, -3.0e38))
                link(dve.max(out_v[:, 8:16], work))
                dve.max_index(out_i[:, 0:8], out_v[:, 0:8], values)
                return link(dve.max_index(out_i[:, 8:16], out_v[:, 8:16], work))

            def pick(which, temps):
                oh = temps[0].rearrange("p (k j) -> p k j", k=TOPK)
                link(tt(oh, spread(ci[:, 1 + which, :].unsqueeze(2), 2, TOPK),
                        spread(iota[:, :].unsqueeze(1), 1, TOPK), ALU.is_equal))
                link(tt(oh, oh, spread(topi[:, which, :].unsqueeze(1), 1, TOPK), ALU.mult))
                link(dve.tensor_reduce(eh[:, which, :], oh, AX.X, ALU.add))

            def choose(scores, temps, hh, chosen, step):
                less, sums = temps
                mine = slice(TOPK * hh, TOPK * hh + TOPK)
                if step == 0:
                    top16(scores[0], less[:, 0:P], tops[:, 0, :], topi[:, 0, :])
                if step == 1:
                    top16(scores[1], less[:, P:2 * P], tops[:, 1, :], topi[:, 1, :])
                    tt(sums.rearrange("p (a b) -> p a b", a=TOPK), spread(tops[:, 0, :].unsqueeze(2), 2, TOPK),
                       spread(tops[:, 1, :].unsqueeze(1), 1, TOPK), ALU.add).then_inc(s_topk, 1)
                if step == 2:
                    dve.wait_ge(s_topk, chosen)
                    held()
                    top16(sums, less, gate[:, mine], ci[:, 0, :])
                    ts(gmax[:, hh:hh + 1], gate[:, TOPK * hh:TOPK * hh + 1], -1.0, None, ALU.mult).then_inc(s_gmax, 1)
                if step == 3:
                    ts(ci[:, 1, :], ci[:, 0, :], 4, None, ALU.logical_shift_right)
                    link(ts(ci[:, 2, :], ci[:, 0, :], TOPK - 1, None, ALU.bitwise_and))
                    pick(0, temps)
                if step == 4:
                    pick(1, temps)
                    stt(idx[:, mine], eh[:, 0, :], float(P), eh[:, 1, :], ALU.mult, ALU.add).then_inc(s_sel, 1)

            def query(b, head, step, tick):
                step -= 4
                if not 0 <= step < 5:
                    return
                if step < 2:
                    dve.wait_ge(s_score, b * 16 + 2 * head + 1 + step)
                    held()
                if step == 4:
                    if tick >= TOPK and head > 0:
                        dve.wait_ge(s_acc0, streams_before(b) + 1)
                    elif not is_count(b, 0):
                        dve.wait_ge(s_vsum, experts_before(b - 1) + TOPK * head + TOPK)
                pair_of = [bank[2 * (head % 2) + half][:, 0:P] for half in range(2)]
                choose(pair_of, choice, head, heads_before(b) + head + 1, step)

            def query_sample(tick):
                for group in range(2):
                    step = tick - (T_SAMPLE_Q + 8 * group + 12)
                    if 0 <= step < 5:
                        if step == 0:
                            dve.wait_ge(s_score_s, group + 1)
                        pair_of = [acc[:, 512 * group + P * half:512 * group + P * half + P] for half in range(2)]
                        choose(pair_of, choice_s, PEER_HEADS - 2 + group, group + 1, step)

            def mixer(v, w, n, full, tick):
                if tick in (T_CONV, T_CONV + 1):
                    if tick == T_CONV:
                        dve.wait_ge(s_xl, v + 1)
                    for j in range(CONV_W // 2):
                        j += CONV_W // 2 * (tick - T_CONV)
                        for f in range(FT):
                            src = xl[:, f, j:j + n]
                            if j == 0:
                                last = ts(xc[:, f, 0:n], src, cw[:, f, 0:1], vec[:, convb][:, f:f + 1], ALU.mult, ALU.add)
                            else:
                                last = stt(xc[:, f, 0:n], src, cw[:, f, j:j + 1], xc[:, f, 0:n], ALU.mult, ALU.add)
                        if j < CONV_W - 1:
                            link(last)
                        else:
                            last.then_inc(s_xc, 1)
                if tick == T_CONV + 2:
                    dve.wait_ge(s_xc, v + 1)
                    link(dve.tensor_copy(xl[:, :, 0:CONV_W - 1], xl[:, :, n:n + CONV_W - 1]))
                if tick == T_ROWS:
                    dve.wait_ge(s_fneg, v + 1)
                    stt(rows[1][:, 0:n], rows[0][:, 0:n], -1.0, rows[0][:, 0:n], ALU.mult, ALU.max).then_inc(s_fabs, 1)
                if tick == T_ROWS + 2:
                    dve.wait_ge(s_fln, v + 1)
                    link(stt(rows[1][:, 0:n], rows[0][:, 0:n], 0.0, rows[1][:, 0:n], ALU.max, ALU.add))
                    link(dve.tensor_tensor_scan(rows[2][:, 0:n], ones4[:, 0:n], rows[1][:, 0:n], 0.0, ALU.mult, ALU.subtract))
                    link(stt(rows[3][:, 0:n], bB[0:HEADS, 0:n], bg[:, 0:1], rows[2][:, 0:n], ALU.add, ALU.subtract))
                    link(dve.tensor_tensor_scan(rows[4][:, 0:n], rows[3][:, 0:n], rows[3][:, 0:n], mst[:, :], ALU.max, ALU.max))
                    ts(rows[5][:, 0:n], rows[4][:, 0:n], -1.0, None, ALU.mult)
                    tt(rows[0][:, 0:n], rows[2][:, 0:n], rows[4][:, 0:n], ALU.add).then_inc(s_mrow, 1)
                if full and tick == T_GELU + 1:
                    dve.wait_ge(s_gl, w + 1)
                    link(ts(t3[:, :, 0:n], t3[:, :, 0:n], GELU_CUBIC, 1.0, ALU.mult, ALU.add))
                    link(tt(t3[:, :, 0:n], t3[:, :, 0:n], G[:, :, 0:n], ALU.mult))
                    ts(t3[:, :, 0:n], t3[:, :, 0:n], -50.0, None, ALU.max).then_inc(s_gl_arg, 1)
                if full and tick == T_GELU + 3:
                    dve.wait_ge(s_gl_exp, w + 1)
                    link(ts(t3[:, :, 0:n], t3[:, :, 0:n], 1.0, None, ALU.add))
                    link(dve.reciprocal(t3[:, :, 0:n], t3[:, :, 0:n]))
                    link(tt(G[:, :, 0:n], G[:, :, 0:n], t3[:, :, 0:n], ALU.mult))
                if tick == T_ROWS + 4:
                    dve.wait_ge(s_rows, v + 1)
                    link(dve.tensor_copy(mst[:, :], rows[0][:, n - 1:n]))
                    ts(dg4[:, :], ident[0:HEADS, 0:HEADS], rows[4][:, n - 1:n], None, ALU.mult).then_inc(s_dg, 1)
                if tick == T_LRU + 2:
                    dve.wait_ge(s_ri_exp, v + 1)
                    link(ts(t1[:, :, 0:n], t1[:, :, 0:n], 1.0, None, ALU.add))
                    dve.reciprocal(t1[:, :, 0:n], t1[:, :, 0:n]).then_inc(s_r, 1)
                if tick == T_LRU + 3:
                    link(ts(t2[:, :, 0:n], t2[:, :, 0:n], 1.0, None, ALU.add))
                    link(dve.reciprocal(t2[:, :, 0:n], t2[:, :, 0:n]))
                if tick == T_LRU + 4:
                    dve.wait_ge(s_r, v + 1)
                    link(tt(t4[:, :, 0:n], t1[:, :, 0:n], spread(decay_c[:, FT:2 * FT].unsqueeze(2), 2, n), ALU.mult))
                    tt(t2[:, :, 0:n], t2[:, :, 0:n], xc[:, :, 0:n], ALU.mult)
                if tick == T_LRU + 5:
                    link(ts(by4(bC)[:, :, 0:n], t4[:, :, 0:n], 1.0 / 120, None, ALU.mult))
                for at, c in ((5, -1.0 / 24), (6, 1.0 / 6), (6, -0.5), (7, 1.0)):
                    if tick == T_LRU + at:
                        link(stt(by4(bC)[:, :, 0:n], by4(bC)[:, :, 0:n], c, t4[:, :, 0:n], ALU.add, ALU.mult))
                if tick == T_LRU + 7:
                    link(ts(t4[:, :, 0:n].bitcast(u32), t4[:, :, 0:n], 0.125, None, ALU.is_lt))
                if tick == T_LRU + 8:
                    dve.wait_ge(s_a, v + 1)
                    link(tt(t1[:, :, 0:n], t3[:, :, 0:n], t3[:, :, 0:n], ALU.mult))
                    link(ts(t1[:, :, 0:n], t1[:, :, 0:n], -1.0, 1.0, ALU.mult, ALU.add))
                if tick == T_LRU + 9:
                    link(dve.copy_predicated(t1[:, :, 0:n], t4[:, :, 0:n].bitcast(u32), by4(bC)[:, :, 0:n]))
                    ts(t1[:, :, 0:n], t1[:, :, 0:n], 2.0 ** -60, None, ALU.max).then_inc(s_m2, 1)
                if tick == T_LRU + 11:
                    dve.wait_ge(s_mult, v + 1)
                    if is_count(v, 1):
                        link(dve.memset(t1[:, :, 0:1], 1.0))
                    link(tt(t2[:, :, 0:n], t2[:, :, 0:n], t1[:, :, 0:n], ALU.mult))
                    for f in range(FT):
                        last = dve.tensor_tensor_scan(t4[:, f, 0:n], t3[:, f, 0:n], t2[:, f, 0:n], hst[:, f:f + 1], ALU.mult, ALU.add)
                    link(last)
                if tick == T_LRU + 12:
                    last = dve.tensor_copy(hst[:, :].unsqueeze(2), t4[:, :, n - 1:n])
                    if full:
                        last = tt(G[:, :, 0:n], G[:, :, 0:n], t4[:, :, 0:n], ALU.mult)
                    last.then_inc(s_lru, 1)
                if tick == T_V + 7:
                    dve.wait_ge(s_kt_ps, v + 1)
                    dve.wait_ge(s_cols, v + 1)
                    mine = tokens_of(v, n)
                    tt(kw[mine, :, :], by4(bF)[mine, :, :], spread(cols[mine, 2, :].unsqueeze(2), 2, HEAD), ALU.mult).then_inc(s_kw, 1)
                if full and tick == T_CHUNK + 1:
                    dve.wait_ge(s_bc_ps, w + 1)
                    tt(t3[0:n, :, 0:n], by4(bA)[0:n, :, 0:n], spread(mask[0:n, 0:n].unsqueeze(1), 1, HEADS), ALU.add).then_inc(s_wmask, 1)
                    dve.wait_ge(s_q, w + 1)
                    tt(t2[:, :, 0:n], by4(bB)[:, :, 0:n], qT[:, :, 0:n], ALU.mult).then_inc(s_qd, 1)
                if full and tick == T_CHUNK + 5:
                    dve.wait_ge(s_w, w + 1)
                    dve.wait_ge(s_s_ps, w + 1)
                    tt(t3[0:n, :, 0:n], t3[0:n, :, 0:n], by4(bC)[0:n, :, 0:n], ALU.mult).then_inc(s_p, 1)
                if full and tick == T_CHUNK + 9:
                    dve.wait_ge(s_num_ps, w + 1)
                    for b in range(2):
                        last = dve.tensor_copy(den[0:n, 2 * b:2 * b + 2].unsqueeze(2), pair(bank[b])[0:n, :, HEAD:HEAD + 1])
                    link(last)
                    link(stt(den[0:n, :], den[0:n, :], -1.0, den[0:n, :], ALU.mult, ALU.max))
                    link(tt(den[0:n, :], den[0:n, :], cols[0:n, 1, :], ALU.max))
                    link(dve.reciprocal(den[0:n, :], den[0:n, :]))
                    for b in range(2):
                        last = tt(t1[0:n, 2 * b:2 * b + 2, :], pair(bank[b])[0:n, :, 0:HEAD],
                                  spread(den[0:n, 2 * b:2 * b + 2].unsqueeze(2), 2, HEAD), ALU.mult)
                    last.then_inc(s_num, 1)
                if full and tick == T_CHUNK + 10:
                    dve.wait_ge(s_num, w + 1)
                    link(tt(t4[0:n, :, :], t1[0:n, :, :], t1[0:n, :, :], ALU.mult))
                    dve.tensor_reduce(hstat[0:n, :], t4[0:n, :, :], AX.X, ALU.add).then_inc(s_hsq, 1)
                if tick == T_CHUNK + 11:
                    dve.wait_ge(s_c_ps, v + 1)
                    for f in range(HEADS):
                        last = stt(C[:, f, :], C[:, f, :], cols[:, 4, f:f + 1], pair(bank[2 + f // 2])[:, f % 2, :], ALU.mult, ALU.add)
                    last.then_inc(s_c, 1)
                if not full:
                    return
                if tick == T_CHUNK + 13:
                    dve.wait_ge(s_o, w + 1)
                    link(ts(sigo[0:n, :, :], sigo[0:n, :, :], 1.0, None, ALU.add))
                    link(dve.reciprocal(sigo[0:n, :, :], sigo[0:n, :, :]))
                if tick == T_CHUNK + 14:
                    link(tt(t1[0:n, :, :], t1[0:n, :, :], sigo[0:n, :, :], ALU.mult))
                    dve.wait_ge(s_hrs, w + 1)
                    tt(t1[0:n, :, :], t1[0:n, :, :], spread(hstat[0:n, :].unsqueeze(2), 2, HEAD), ALU.mult).then_inc(s_ym, 1)
                if tick == T_NORM2:
                    dve.wait_ge(s_out_ps, w + 1)
                    dve.wait_ge(s_xn, projected(v))
                    for half in range(2):
                        last = tt(h[0:n, 512 * half:512 * half + 512], bank[half][0:n, :], h[0:n, 512 * half:512 * half + 512], ALU.add)
                    last.then_inc(s_h2, 1)
                if tick == T_NORM2 + 2:
                    if is_count(v, 0):
                        dve.wait_ge(s_rows_bc, 32)
                    dve.wait_ge(s_rstd2, w + 1)
                    stt(xn[0:n, :], h[0:n, :], stat[0:n, 5:6], ffn_bc[0:n, :], ALU.mult, ALU.mult).then_inc(s_xn2, 1)

            def dot(b, e):
                slot, arrived = row_of(0, b, e)
                if e == 0:
                    dve.wait_ge(s_xcur, streams_before(b) + 1)
                dve.wait_ge(s_row[slot], arrived)
                row = ring[:, slot, :]
                stt(row, row, 1.0, xcur[:, :], ALU.mult, ALU.mult, accum_out=dots[:, column(b, e):column(b, e) + 1]).then_inc(s_dot, 1)

            def gelu_arg(b, g):
                first = column(b, TOPK * g)
                d = dots[:, first:first + TOPK]
                dve.wait_ge(s_dot, experts_before(b) + TOPK * g + TOPK)
                link(tt(gl_a[:, :], d, d, ALU.mult))
                link(ts(gl_a[:, :], gl_a[:, :], GELU_CUBIC, 1.0, ALU.mult, ALU.add))
                link(tt(gl_a[:, :], gl_a[:, :], d, ALU.mult))
                ts(gl_a[:, :], gl_a[:, :], -50.0, None, ALU.max).then_inc(s_arg, 1)
                dve.wait_ge(s_gate, heads_before(b) + g + 1)
                link(dve.reciprocal(ginv[:, :], gsum[:, first // TOPK:first // TOPK + 1]))
                link(stt(gl_b[:, :], d, ginv[:, :], gate[:, first:first + TOPK], ALU.mult, ALU.mult))

            def coefficients(b, g):
                dve.wait_ge(s_gexp, heads_before(b) + g + 1)
                link(ts(gl_a[:, :], gl_a[:, :], 1.0, None, ALU.add))
                link(dve.reciprocal(gl_a[:, :], gl_a[:, :]))
                tt(coef[:, column(b, TOPK * g):column(b, TOPK * g) + TOPK], gl_a[:, :], gl_b[:, :], ALU.mult).then_inc(s_coef, 1)

            def dots_of(b, e):
                dot(b, e)
                if e % TOPK == TOPK - 1:
                    gelu_arg(b, e // TOPK)

            def finish(b):
                n = n_experts(b)
                dve.wait_ge(s_rstd_y, streams_before(b) + 1)
                y = xn[0:n, :]
                stt(y, y, stat[0:n, 8:9], final_bc[0:n, :], ALU.mult, ALU.mult).then_inc(s_y, 1)

            def beside(b, tick, more):
                for head in range(1, PEER_HEADS):
                    query(b, head, tick - T_QUERY - QUERY_TICKS * (head - 1), tick)
                if more:
                    mixer(b + 3, b + 2, P, True, tick)
                    query(b + 1, 0, tick - T_QUERY0, tick)

            dve.wait_ge(s_const, 7)
            setup()
            for tick in range(T_MIXER, BLOCK_TICKS):
                mixer(0, 0, SAMPLE, True, tick)
            dve.wait_ge(s_state_out, 64)
            dve.memset(xl[:, :, 0:CONV_W - 1], 0.0)
            dve.memset(hst[:, :], 0.0)
            dve.memset(C[:, :, :], 0.0)
            dve.memset(mst[:, :], 0.0).then_inc(s_reset, 1)
            dve.wait_ge(s_reset, 1)
            for tick in range(T_MIXER, BLOCK_TICKS):
                mixer(1, 1, META, False, tick)
                query_sample(tick)
            for e in range(TOPK):
                dots_of(None, e)
            for step in range(TOPK + MIXER_LEAD):
                if step == MIXER_LEAD:
                    coefficients(None, 0)
                if step >= MIXER_LEAD:
                    dots_of(None, TOPK + step - MIXER_LEAD)
                for t in range(T_MIXER + MIXER_PACE * step, T_MIXER + MIXER_PACE * (step + 1)):
                    mixer(2, 1, P, True, t)
                    query(0, 0, t - T_QUERY0, t)
            for tick in range(TOPK):
                dots_of(0, tick)
                if tick == 0:
                    coefficients(None, 1)
                beside(0, tick, False)
            finish(None)
            with dve.Fori(0, BLOCKS - 1) as b:
                restart()
                for tick in range(TOPK, BLOCK_TICKS):
                    if tick % TOPK == 0:
                        coefficients(b, tick // TOPK - 1)
                    dots_of(b, tick)
                    beside(b, tick, True)
                for tick in range(TOPK):
                    if tick == 0:
                        coefficients(b, PEER_HEADS - 1)
                    dots_of(b + 1, tick)
                    beside(b + 1, tick, False)
                finish(b)
            restart()
            b = BLOCKS - 1
            for tick in range(TOPK, BLOCK_TICKS):
                if tick % TOPK == 0:
                    coefficients(b, tick // TOPK - 1)
                dots_of(b, tick)
                beside(b, tick, False)
            coefficients(b, PEER_HEADS - 1)
            finish(b)


def kernel(**inputs):
    import concourse.bacc as bacc
    from concourse.bass_utils import run_bass_kernel_spmd

    a = {k: np.asarray(v) for k, v in inputs.items()}

    def channels(x):
        x = x.reshape(x.shape[0], -1, P)
        return np.ascontiguousarray(x.transpose(2, 1, 0))

    def halves(x):
        return np.ascontiguousarray(x.reshape(FT, 2, 64, 64).transpose(1, 2, 0, 3))

    vectors = [a[k][0] for k in ("lru_ba", "lru_bx", "lru_lambda", "mlstm_norm", "conv_b", "norm_mix")]
    ins = {
        "x_prompt": a["x_prompt"][0],
        "x_sample": a["x_sample"][0],
        "meta": a["meta_tokens"],
        "w_in": a["w_in"][0],
        "vecs": np.concatenate([v.reshape(-1, P).T for v in vectors], axis=1),
        "conv_w": channels(a["conv_w"][0]),
        "b_gates": a["b_gates"][0].reshape(2, HEADS).T,
        "lru_wa": halves(a["lru_wa"][0]),
        "lru_wx": halves(a["lru_wx"][0]),
        "w_out": a["w_out"][0],
        "ffn_row": a["norm_ffn"],
        "final_row": a["norm_final"][None],
        "wq": a["peer_wq"][0].reshape(CM, P, 2 * PEER_HEADS, P).transpose(2, 1, 0, 3),
        "keys": np.stack([a["peer_keys1"][0].T, a["peer_keys2"][0].T], axis=1),
        "peer_u": a["peer_u"][0],
        "peer_v": a["peer_v"][0],
        "conv0": channels(a["state_conv"][0, 0]),
        "lru0": a["state_lru"][0, 0].reshape(FT, P).T,
        "c0": np.concatenate([a["state_mlstm_c"][0, 0].transpose(1, 0, 2), a["state_mlstm_n"][0, 0].T[:, :, None]], axis=2),
        "m0": a["state_mlstm_m"][0, 0][:, None],
    }
    ins = {k: np.ascontiguousarray(v) for k, v in ins.items()}
    outs = {
        "y_prompt": (SEQ, D_MODEL),
        "y_sample": (SAMPLE, D_MODEL),
        "conv_out": (2, P, FT, CONV_W - 1),
        "lru_out": (2, P, FT),
        "c_out": (2, P, HEADS, HEAD + 1),
        "m_out": (2, HEADS, 1),
    }
    nc = bacc.Bacc("TRN2", target_bir_lowering=False, num_devices=1, dynamic_dma_scratch_size=4096)
    fp32 = mybir.dt.float32
    aps = [nc.dram_tensor(k, v.shape, fp32, kind="ExternalInput").ap() for k, v in ins.items()]
    aps += [nc.dram_tensor(k, s, fp32, kind="ExternalOutput").ap() for k, s in outs.items()]
    program(nc, *aps)
    r = run_bass_kernel_spmd(nc, [ins], core_ids=[0]).results[0]

    def states(s):
        return (r["conv_out"][s].transpose(2, 1, 0).reshape(1, 1, CONV_W - 1, D_LRU),
                r["lru_out"][s].T.reshape(1, 1, D_LRU),
                r["c_out"][s][:, :, 0:HEAD].transpose(1, 0, 2)[None, None],
                r["c_out"][s][:, :, HEAD].T[None, None],
                r["m_out"][s].reshape(1, 1, HEADS))

    out = (r["y_prompt"][None], r["y_sample"][None], *states(1), *states(0))
    return tuple(np.ascontiguousarray(x) for x in out)
```
